# Optimizing a Trainium2 kernel written in Bass

```python
import math
import jax, jax.numpy as jnp
from jax import lax
import numpy as np

D_MODEL = 1024
BATCH = 1
SEQ = 1024
DEPTH = 1

HEAD_DIM = 64
SB_HEADS = 8
DIFF_HEADS = 4
SB_WIDTH = SB_HEADS * HEAD_DIM
DIFF_QK_WIDTH = DIFF_HEADS * 2 * HEAD_DIM
DIFF_V_WIDTH = DIFF_HEADS * 2 * HEAD_DIM
N_BRANCHES = 2
IN_WIDTH = 3 * SB_WIDTH + 2 * DIFF_QK_WIDTH + DIFF_V_WIDTH + N_BRANCHES * D_MODEL
D_FF = 4 * D_MODEL
BLOCK_Q = 128
ROPE_THETA = 10000.0
LN_EPS = 1e-5
RMS_EPS = 1e-5
DEEPNORM_ALPHA = (2.0 * DEPTH) ** 0.25
DEEPNORM_BETA = (8.0 * DEPTH) ** -0.25

kernel_name = "hybrid_stickbreak_diffattn_gated_deepnorm"

def _lambda_init(layer_idx):
    return 0.8 - 0.6 * math.exp(-0.3 * layer_idx)

def _layer_norm(x, gain, bias):
    xf = x.astype(jnp.float32)
    mu = jnp.mean(xf, axis=-1, keepdims=True)
    var = jnp.mean(jnp.square(xf - mu), axis=-1, keepdims=True)
    y = (xf - mu) * lax.rsqrt(var + LN_EPS) * gain.astype(jnp.float32) + bias.astype(jnp.float32)
    return y.astype(x.dtype)

def _rms_norm(x, gain):
    xf = x.astype(jnp.float32)
    y = xf * lax.rsqrt(jnp.mean(jnp.square(xf), axis=-1, keepdims=True) + RMS_EPS) * gain.astype(jnp.float32)
    return y.astype(x.dtype)

def _rope_tables(seq, dim, dtype):
    inv_freq = ROPE_THETA ** (-jnp.arange(0, dim, 2, dtype=jnp.float32) / dim)
    ang = jnp.arange(seq, dtype=jnp.float32)[:, None] * inv_freq[None, :]
    return jnp.cos(ang).astype(dtype), jnp.sin(ang).astype(dtype)

def _rope(x, cos, sin):
    x1, x2 = jnp.split(x, 2, axis=-1)
    return jnp.concatenate([x1 * cos - x2 * sin, x2 * cos + x1 * sin], axis=-1)

def _stick_breaking_attention(q, k, v):
    s_len = q.shape[2]
    blk = min(BLOCK_Q, s_len)
    scale = q.shape[-1] ** -0.5
    outs = []
    for start in range(0, s_len, blk):
        end = start + blk
        qpos = start + jnp.arange(blk)
        kpos = jnp.arange(end)
        mask = kpos[None, :] < qpos[:, None]
        z = jnp.einsum('bhqd,bhkd->bhqk', q[:, :, start:end], k[:, :, :end]).astype(jnp.float32) * scale
        log_beta = jax.nn.log_sigmoid(z)
        log_1m_beta = jnp.where(mask, jax.nn.log_sigmoid(-z), 0.0)
        suffix = lax.cumsum(log_1m_beta, axis=3, reverse=True) - log_1m_beta
        a = jnp.where(mask, jnp.exp(log_beta + suffix), 0.0)
        outs.append(jnp.einsum('bhqk,bhkd->bhqd', a.astype(v.dtype), v[:, :, :end]))
    return jnp.concatenate(outs, axis=2)

def _differential_attention(q1, q2, k1, k2, v, lam):
    s_len = q1.shape[2]
    blk = min(BLOCK_Q, s_len)
    scale = q1.shape[-1] ** -0.5
    outs = []
    for start in range(0, s_len, blk):
        end = start + blk
        qpos = start + jnp.arange(blk)
        kpos = jnp.arange(end)
        mask = kpos[None, :] <= qpos[:, None]
        z1 = jnp.einsum('bhqd,bhkd->bhqk', q1[:, :, start:end], k1[:, :, :end]).astype(jnp.float32) * scale
        z2 = jnp.einsum('bhqd,bhkd->bhqk', q2[:, :, start:end], k2[:, :, :end]).astype(jnp.float32) * scale
        p1 = jax.nn.softmax(jnp.where(mask, z1, -jnp.inf), axis=-1)
        p2 = jax.nn.softmax(jnp.where(mask, z2, -jnp.inf), axis=-1)
        w = p1 - lam * p2
        outs.append(jnp.einsum('bhqk,bhkd->bhqd', w.astype(v.dtype), v[:, :, :end]))
    return jnp.concatenate(outs, axis=2)

def setup_inputs(seed: int = 0) -> dict:
    key = jax.random.key(seed)
    ks = jax.random.split(key, 17)
    f32 = jnp.float32

    def dense(k, shape, fan_in, gain=1.0):
        return jax.random.normal(k, shape, f32) * (fan_in ** -0.5) * gain

    x = jax.random.normal(ks[0], (BATCH, SEQ, D_MODEL), f32)
    w_in = dense(ks[1], (DEPTH, D_MODEL, IN_WIDTH), D_MODEL)
    col_gain = np.ones((IN_WIDTH,), np.float32)
    col_gain[2 * SB_WIDTH:3 * SB_WIDTH] = DEEPNORM_BETA
    v_b_start = 3 * SB_WIDTH + 2 * DIFF_QK_WIDTH
    col_gain[v_b_start:v_b_start + DIFF_V_WIDTH] = DEEPNORM_BETA
    w_in = w_in * jnp.asarray(col_gain)
    w_branch_a = dense(ks[2], (DEPTH, SB_WIDTH, D_MODEL), SB_WIDTH, DEEPNORM_BETA)
    w_branch_b = dense(ks[3], (DEPTH, DIFF_V_WIDTH, D_MODEL), DIFF_V_WIDTH, DEEPNORM_BETA)
    w_out = dense(ks[4], (DEPTH, D_MODEL, D_MODEL), D_MODEL, DEEPNORM_BETA)
    lambda_q1 = 0.1 * jax.random.normal(ks[5], (DEPTH, HEAD_DIM), f32)
    lambda_k1 = 0.1 * jax.random.normal(ks[6], (DEPTH, HEAD_DIM), f32)
    lambda_q2 = 0.1 * jax.random.normal(ks[7], (DEPTH, HEAD_DIM), f32)
    lambda_k2 = 0.1 * jax.random.normal(ks[8], (DEPTH, HEAD_DIM), f32)
    subln_gain = 1.0 + 0.02 * jax.random.normal(ks[9], (DEPTH, 2 * HEAD_DIM), f32)
    ln1_gain = 1.0 + 0.02 * jax.random.normal(ks[10], (DEPTH, D_MODEL), f32)
    ln1_bias = 0.02 * jax.random.normal(ks[11], (DEPTH, D_MODEL), f32)
    w_ff1 = dense(ks[12], (DEPTH, D_MODEL, D_FF), D_MODEL, DEEPNORM_BETA)
    w_ff2 = dense(ks[13], (DEPTH, D_FF, D_MODEL), D_FF, DEEPNORM_BETA)
    ln2_gain = 1.0 + 0.02 * jax.random.normal(ks[14], (DEPTH, D_MODEL), f32)
    ln2_bias = 0.02 * jax.random.normal(ks[15], (DEPTH, D_MODEL), f32)
    return {"x": x, "w_in": w_in, "w_branch_a": w_branch_a, "w_branch_b": w_branch_b, "w_out": w_out,
            "lambda_q1": lambda_q1, "lambda_k1": lambda_k1, "lambda_q2": lambda_q2, "lambda_k2": lambda_k2,
            "subln_gain": subln_gain, "ln1_gain": ln1_gain, "ln1_bias": ln1_bias,
            "w_ff1": w_ff1, "w_ff2": w_ff2, "ln2_gain": ln2_gain, "ln2_bias": ln2_bias}

def reference(x, w_in, w_branch_a, w_branch_b, w_out, lambda_q1, lambda_k1, lambda_q2, lambda_k2,
              subln_gain, ln1_gain, ln1_bias, w_ff1, w_ff2, ln2_gain, ln2_bias):
    b, s, _ = x.shape
    cos, sin = _rope_tables(s, HEAD_DIM, x.dtype)
    c_qa, c_ka, c_va = SB_WIDTH, 2 * SB_WIDTH, 3 * SB_WIDTH
    c_qb = c_va + DIFF_QK_WIDTH
    c_kb = c_qb + DIFF_QK_WIDTH
    c_vb = c_kb + DIFF_V_WIDTH
    c_ga = c_vb + D_MODEL
    for l in range(DEPTH):
        lam_init = _lambda_init(l)
        proj = jnp.einsum('bsd,de->bse', x, w_in[l])

        def heads(t, n_heads):
            return t.reshape(b, s, n_heads, -1).transpose(0, 2, 1, 3)

        qa = heads(proj[..., :c_qa], SB_HEADS)
        ka = heads(proj[..., c_qa:c_ka], SB_HEADS)
        va = heads(proj[..., c_ka:c_va], SB_HEADS)
        ya = _stick_breaking_attention(qa, ka, va)
        ya = ya.transpose(0, 2, 1, 3).reshape(b, s, SB_WIDTH)

        qb = proj[..., c_va:c_qb].reshape(b, s, DIFF_HEADS, 2, HEAD_DIM).transpose(0, 2, 3, 1, 4)
        kb = proj[..., c_qb:c_kb].reshape(b, s, DIFF_HEADS, 2, HEAD_DIM).transpose(0, 2, 3, 1, 4)
        vb = heads(proj[..., c_kb:c_vb], DIFF_HEADS)
        q1, q2 = _rope(qb[:, :, 0], cos, sin), _rope(qb[:, :, 1], cos, sin)
        k1, k2 = _rope(kb[:, :, 0], cos, sin), _rope(kb[:, :, 1], cos, sin)
        lam = (jnp.exp(jnp.sum(lambda_q1[l].astype(jnp.float32) * lambda_k1[l].astype(jnp.float32)))
               - jnp.exp(jnp.sum(lambda_q2[l].astype(jnp.float32) * lambda_k2[l].astype(jnp.float32)))
               + lam_init)
        yb = _differential_attention(q1, q2, k1, k2, vb, lam)
        yb = _rms_norm(yb, subln_gain[l]) * (1.0 - lam_init)
        yb = yb.transpose(0, 2, 1, 3).reshape(b, s, DIFF_V_WIDTH)

        gate_a = jax.nn.sigmoid(proj[..., c_vb:c_ga])
        gate_b = jax.nn.sigmoid(proj[..., c_ga:])
        merged = (gate_a * jnp.einsum('bse,ed->bsd', ya, w_branch_a[l])
                  + gate_b * jnp.einsum('bse,ed->bsd', yb, w_branch_b[l]))
        mix_out = jnp.einsum('bsd,de->bse', merged, w_out[l])
        x = _layer_norm(DEEPNORM_ALPHA * x + mix_out, ln1_gain[l], ln1_bias[l])

        h = jnp.square(jax.nn.relu(jnp.einsum('bsd,df->bsf', x, w_ff1[l])))
        ff_out = jnp.einsum('bsf,fd->bsd', h, w_ff2[l])
        x = _layer_norm(DEEPNORM_ALPHA * x + ff_out, ln2_gain[l], ln2_bias[l])
    return x


_drawn_inputs = setup_inputs


def setup_inputs(seed=0):
    import zlib

    import numpy as np

    out = dict(_drawn_inputs(seed))
    spreads = {}
    factors = {'lambda_q1': 200.0,
     'lambda_k1': 5.066,
     'lambda_q2': 7.383,
     'lambda_k2': 8.0,
     'subln_gain': 27.045,
     'ln1_gain': 8.082,
     'ln1_bias': 7.798,
     'ln2_gain': 23.935,
     'ln2_bias': 23.699,
     'w_branch_a': 2.901}
    for name, (base, spread) in spreads.items():
        noise = np.random.default_rng([zlib.crc32(name.encode()), seed]).standard_normal(out[name].shape)
        drawn = base * np.exp(spread * noise) if base else spread * noise
        out[name] = __import__('jax').numpy.asarray(drawn.astype(out[name].dtype))
    for name, factor in factors.items():
        out[name] = (out[name] * factor).astype(out[name].dtype)
    return out
```

```python
from contextlib import ExitStack

import numpy as np

import concourse.bass as bass
from concourse import mybir

F32 = mybir.dt.float32
F32R = mybir.dt.float32r
ALU = mybir.AluOpType
ACT = mybir.ActivationFunctionType
AX_X = mybir.AxisListType.X

P = 128
D = 1024
S = 1024
HD = 64
KT = D // P
TB = S // P
NH = 512
FF = 4096
SB_GROUPS = 4
GROUPS = 8
SCALE = HD ** -0.5
ALPHA = 2.0 ** 0.25
EPS = 1e-5
LAM_INIT = 0.8 - 0.6
BIG = 3.0e38

SB_W = 512
GATE_A = 6 * SB_W
GATE_B = GATE_A + D

SB_UNITS = 16
DF_UNITS = 8
SB_BATCH = [(u, b) for u in range(SB_UNITS) for b in range((u // 2) // 4 + 1)]
DF_BATCH = [(u, b) for u in range(DF_UNITS) for b in range(u // 4 + 1)]


def const_arrays():
    q = np.arange(P)[:, None]
    k = np.arange(P)[None, :]
    ident = (q == k).astype(np.float32)
    strict = (k < q).astype(np.float32)
    cap = np.where(k <= q, np.float32(BIG), np.float32(-BIG)).astype(np.float32)
    inv = np.float32(10000.0) ** (-np.arange(0, HD, 2, dtype=np.float32) / np.float32(HD))
    ang = np.arange(S, dtype=np.float32)[:, None] * inv[None, :].astype(np.float32)
    cos, sin = np.cos(ang).astype(np.float32).T, np.sin(ang).astype(np.float32).T
    rows_c = np.concatenate([cos] * 4, axis=0)
    rows_s = np.concatenate([-sin, sin, -sin, sin], axis=0)
    small = np.concatenate([ident, strict, 1.0 - strict, cap], axis=1).astype(np.float32)
    return small, np.stack([rows_c, rows_s], axis=1).astype(np.float32)


def span(qb, b):
    total = qb + 1
    if total <= 4:
        return 0, total, True
    half = (total + 1) // 2
    return (0, half, False) if b == 0 else (half, total - half, True)


class Group:

    def __init__(self, g, sb, tiles, rope):
        self.g, self.sb, self.tiles, self.rope = g, sb, tiles, rope
        self.batches = SB_BATCH if sb else DF_BATCH
        self.nunits = SB_UNITS if sb else DF_UNITS
        total = 48 * tiles
        self.head = 34 if sb else 38
        single = (sum(1 for v, _ in self.batches if v == u) == 1 for u, _ in self.batches)
        share = (6, 2.5, 5.5) if sb else (13, 6.5, 6.5)
        weight = np.cumsum([share[0] if one else share[1 + b] for one, (_, b) in zip(single, self.batches)])
        self.until = [int(self.head + w * (total - self.head) // weight[-1]) for w in weight]

    def z(self, j):
        return self.g * 16 + j

    def unit(self, u):
        return self.g * 16 + u if self.sb else self.g * 8 + (u + 32)

    def tr(self, k):
        return self.g * 26 + k if self.sb else self.g * 14 + (k + 48)

    def tile(self, t):
        return self.g * 3 + (3 + t)

    def plain(self, t, h):
        if not self.rope:
            if isinstance(self.g, int) and self.g == GROUPS - 1:
                return 32 + 2 * t + h
            return self.g * 6 + (6 + 2 * t + h)
        return self.g * 2 + (24 - 6 + h)

    def roped(self, t, h):
        return self.g * 4 + (2 * t + h - 12)

    def is_rope(self, t):
        return self.rope and t < 2

    def halves_at(self, k):
        lo = 24 if k == 0 else self.until[k - 1]
        hi = self.until[k]
        return [i for i in range(1, 2 * self.tiles) if lo < 24 * (i + 1) <= hi]


class Chain:

    def __init__(self, eng, sem):
        self.eng, self.sem, self.base, self.n = eng, sem, 0, 0

    def __call__(self, ins):
        ins.then_inc(self.sem, 1)
        self.n += 1

    def sync(self):
        self.eng.wait_ge(self.sem, self.base + self.n)

    def link(self, ins):
        self(ins)
        self.sync()

    def loop(self, start, end, per, body):
        before = self.n
        with self.eng.Fori(start, end) as i:
            self.base, self.n = i * per + (before - start * per), 0
            body(i)
            assert self.n == per, f"the loop's body counts {self.n}, not {per}"
        self.base, self.n = 0, before + per * (end - start)


def layer_kernel(nc, x, w_in, w_branch_a, w_branch_b, w_out, lambda_q1, lambda_k1, lambda_q2,
                 lambda_k2, subln_gain, ln1_gain, ln1_bias, w_ff1, w_ff2, ln2_gain, ln2_bias,
                 consts, rope, out):
    with ExitStack() as ctx:
        base = (nc.sbuf_base + 63) // 64 * 64

        def at(name, kib, shape, dt=F32, off=0):
            return nc.alloc_sbuf_tensor_at(name, shape, dt, offset=base + int(kib * 1024) + off)

        def pb(name, shape):
            return ctx.enter_context(nc.psum_tensor(name, shape, F32))

        def sem(name):
            return ctx.enter_context(nc.semaphore(name))

        xt_h = at("xt_h", 0, [P, KT, S], F32R)
        xt_l = at("xt_l", 32, [P, KT, S], F32R)
        y = at("y", 64, [P, 8, S])
        y_l = at("y_l", 64, [P, 8, S], F32R)
        y_h = at("y_h", 96, [P, 8, S], F32R)
        q_st = [at(f"q_st{m}", 96 + 4 * m, [P, S], F32R) for m in range(2)]
        k_hi = [at(f"k_hi{m}", 104 + 4 * m, [P, S], F32R) for m in range(2)]
        k_lo = [at(f"k_lo{m}", 112 + 4 * m, [P, S], F32R) for m in range(2)]
        v_st = at("v_st", 120, [P, TB, 2, P], F32R)
        v_f = at("v_f", 120, [P, TB, P])
        be = [at(f"be{i}", 128 + 4 * i, [P, S]) for i in range(2)]
        om = [at(f"om{i}", 136 + 4 * i, [P, S]) for i in range(2)]
        sb_be = be + [y[:, 6, :], y[:, 7, :]]
        sb_om = om + [y[:, 4, :], y[:, 5, :]]
        df_e1 = be + [at("e1_2", 124, [P, S])]
        df_e2 = om + [at("e2_2", 148, [P, S])]
        a_t = at("a_t", 144, [P, 2, 4, 2, P], F32R)
        w_t = at("w_t", 144, [P, 2, NH])
        swap = at("swap", 152, [P, NH])
        y_up = at("y_up", 154, [P, 256])
        y_sum = at("y_sum", 155, [P, 256])
        cs = at("cs", 156, [P, 2, S])
        w_raw = at("w_raw", 164, [P, KT, P])
        w_hi = [at(f"w_hi{s}", 168 + 8 * s, [P, KT, P], F32R) for s in range(3)]
        w_lo = [at(f"w_lo{s}", 172 + 8 * s, [P, KT, P], F32R) for s in range(3)]
        stage = [at(f"stage{t}", 192 + 4 * t, [P, S]) for t in range(3)]
        small = at("small", 204, [P, 4, P])
        ident, strict, loose, cap = (small[:, i, :] for i in range(4))
        vecs = at("vecs", 206, [P, 256])
        one, n_lam, g_sub = (vecs[:, i:i + 1] for i in range(3))
        dots, exps = vecs[:, 4:6], vecs[:, 6:8]
        idle = vecs[:, 3:4]
        peak, n_peak, e_sum, e_inv, c_neg = (
            [vecs[:, 8 + 4 * i + 2 * p:10 + 4 * i + 2 * p] for p in range(2)] for i in range(5))
        ss, rs, rs_t, rs_v = (vecs[:, 32 + 32 * i:64 + 32 * i] for i in range(4))
        stats = [vecs[:, 160 + 12 * p:172 + 12 * p] for p in range(2)]
        aggr = [vecs[:, 184 + 2 * p:186 + 2 * p] for p in range(2)]
        ln_v, ln_s, ln_r, ln_t = ([vecs[:, 188 + 4 * i + p:189 + 4 * i + p] for p in range(2)]
                                  for i in range(4))
        lams = at("lams", 154, [P, 4, HD])

        res = at("res", 128, [P, KT, S])
        gains = at("gains", 160, [P, 2, D])
        wo_h = at("wo_h", 64, [P, KT, D], F32R)
        wo_l = at("wo_l", 96, [P, KT, D], F32R)
        wo_raw = at("wo_raw", 168, [P, 2, D])
        m_h = [at(f"m_h{s}", 176 + 8 * s, [P, KT, P], F32R) for s in range(2)]
        m_l = [at(f"m_l{s}", 180 + 8 * s, [P, KT, P], F32R) for s in range(2)]
        rows = [at(f"rows{s}", 192 + 4 * s, [P, D]) for s in range(2)]

        h_h = [[at(f"h_h{c}{t}", 64 + 16 * c + 8 * t, [P, S], F32R) for t in range(2)]
               for c in range(2)]
        h_l = [[at(f"h_l{c}{t}", 68 + 16 * c + 8 * t, [P, S], F32R) for t in range(2)]
               for c in range(2)]
        w1_h = [at(f"w1_h{t}", 96 + 8 * t, [P, KT, P], F32R) for t in range(2)]
        w1_l = [at(f"w1_l{t}", 100 + 8 * t, [P, KT, P], F32R) for t in range(2)]
        w2_h = [at(f"w2_h{t}", 112 + 8 * t, [P, D], F32R) for t in range(2)]
        w2_l = [at(f"w2_l{t}", 116 + 8 * t, [P, D], F32R) for t in range(2)]
        w1_raw = [at(f"w1_raw{t}", 168 + 4 * t, [P, KT, P]) for t in range(2)]
        w2_raw = [at(f"w2_raw{t}", 176 + 4 * t, [P, D]) for t in range(2)]
        relu = at("relu", 184, [P, 2, NH])
        h_f = at("h_f", 188, [P, 2, NH])

        p_proj = pb("p_proj", [P, 2, NH])
        p_z = [pb(f"p_z{i}", [P, S]) for i in range(2)]
        p_tr = pb("p_tr", [P, NH])
        p_av = pb("p_av", [P, NH])
        x_banks = [p_proj[:, 0, :], p_proj[:, 1, :], p_z[0][:, 0:NH], p_z[0][:, NH:S],
                   p_z[1][:, 0:NH], p_z[1][:, NH:S], p_tr[:, :], p_av[:, :]]
        up_banks = [p_proj[:, 0, :], p_proj[:, 1, :], p_tr[:, :], p_av[:, :]]
        dn_banks = [p_z[0][:, 0:NH], p_z[0][:, NH:S], p_z[1][:, 0:NH], p_z[1][:, NH:S]]

        s_const, s_rope, s_lam = sem("s_const"), sem("s_rope"), sem("s_lam")
        s_x = [sem(f"s_x{b}") for b in range(TB)]
        s_one, s_zero = sem("s_one"), sem("s_zero")
        xt_turned, xt_hi, xt_lo = sem("xt_turned"), sem("xt_hi"), sem("xt_lo")
        lam_dots, lam_exps, lam_done = sem("lam_dots"), sem("lam_exps"), sem("lam_done")
        wt_in, wt_hi, wt_lo = sem("wt_in"), sem("wt_hi"), sem("wt_lo")
        pj_done, pj_plain = sem("pj_done"), sem("pj_plain")
        rp_swap, rp_free, rp_sin, rp_done = sem("rp_swap"), sem("rp_free"), sem("rp_sin"), sem("rp_done")
        st_act, st_dve, st_pool = sem("st_act"), sem("st_dve"), sem("st_pool")
        pool_idle = sem("pool_idle")
        qk_done, om_ready, z_read = sem("qk_done"), sem("om_ready"), sem("z_read")
        be_masked, om_even, om_odd, a_even, a_odd = sem("be_masked"), sem("om_even"), sem("om_odd"), sem("a_even"), sem("a_odd")
        pk_ready, a_ready = sem("pk_ready"), sem("a_ready")
        tr_done, tr_hi, tr_read = sem("tr_done"), sem("tr_hi"), sem("tr_read")
        at_used, av_done, av_up, av_read, y_done = (
            sem("at_used"), sem("av_done"), sem("av_up"), sem("av_read"), sem("y_done"))
        sq_ready, ss_done, v_eps, v_root, rs_ready = (
            sem("sq_ready"), sem("ss_done"), sem("v_eps"), sem("v_root"), sem("rs_ready"))
        bc_done, yn_ready = sem("bc_done"), sem("yn_ready")
        ya_split, yb_hi, yb_split = sem("ya_split"), sem("yb_hi"), sem("yb_split")
        gate_ready, br_done, br_read, m_ready = (
            sem("gate_ready"), sem("br_done"), sem("br_read"), sem("m_ready"))
        s_gain1, s_gain2 = sem("s_gain1"), sem("s_gain2")
        wo_in = [sem("wo_in0"), sem("wo_in1")]
        wo_split, wo_done = sem("wo_split"), sem("wo_done")
        mt_hi, mt_lo, o_done, o_read = sem("mt_hi"), sem("mt_lo"), sem("o_done"), sem("o_read")
        row_in = [sem("row_in0"), sem("row_in1")]
        ln_var, ln_root, x1_ready, x1_kept = sem("ln_var"), sem("ln_root"), sem("x1_ready"), sem("x1_kept")
        x1_turned, x1_hi, x1_lo = sem("x1_turned"), sem("x1_hi"), sem("x1_lo")
        w1_in = [sem("w1_in0"), sem("w1_in1")]
        w2_in = [sem("w2_in0"), sem("w2_in1")]
        w1_hi, w1_lo, w2_hi, w2_lo = sem("w1_hi"), sem("w1_lo"), sem("w2_hi"), sem("w2_lo")
        up_done, up_relu, h_ready, h_hi, h_lo = (
            sem("up_done"), sem("up_relu"), sem("h_ready"), sem("h_hi"), sem("h_lo"))
        dn_done, dn_added = sem("dn_done"), sem("dn_added")
        f_ready = sem("f_ready")
        s_out = [sem("s_out0"), sem("s_out1")]
        dve_own = sem("dve_own")

        x_tok = x.rearrange("a (t p) d -> (a t) p d", p=P)
        out_tok = out.rearrange("a (t p) d -> (a t) p d", p=P)
        w_in_v = w_in.rearrange("a (k p) e -> (a p) k e", p=P)
        wa_v = w_branch_a.rearrange("a (k p) e -> (a p) k e", p=P)
        wb_v = w_branch_b.rearrange("a (k p) e -> (a p) k e", p=P)
        wo_v = w_out.rearrange("a (k p) e -> (a k) p e", p=P)
        w1_v = w_ff1.rearrange("a (k p) f -> (a p) k f", p=P)
        w2_v = w_ff2.rearrange("a (k p) e -> (a k) p e", p=P)

        LOOPED = SB_GROUPS - 1
        FC = FF // (2 * P)

        def res_rows(tb):
            return res[:, :, bass.ds(tb * P, P)]

        def res_half(tb, h):
            return res[:, 4 * h:4 * h + 4, bass.ds(tb * P, P)]

        def by_block(ap, n=4):
            return ap.rearrange("p (k c) -> p k c", k=n)

        def apart(eng):
            eng.wait_ge(s_one, 1)

        def wait_stage(eng, g, roped):
            if roped:
                eng.wait_ge(rp_done, g * 4 - 12)
            else:
                eng.wait_ge(pj_plain, g * 6 + 4)
            if not (isinstance(g, int) and g == 0):
                eng.wait_ge(qk_done, g * 16)

        def wait_weights(eng, G, u):
            if G.sb:
                eng.wait_ge((a_even, a_odd)[u % 2], G.g * 8 + (u // 2 + 1))
            else:
                eng.wait_ge(a_ready, G.g * 8 + (u + 1 - 32))

        def stack_part(G, k):
            if isinstance(G.g, int) and G.g == GROUPS - 1:
                return None
            part = k - (19 if G.sb else 8)
            return part if 0 <= part < 3 else None

        def at_free(eng, G, k):
            g = G.g
            ends = [max(i for i, x in enumerate(G.batches) if x[0] == G.batches[i2][0]) == i2
                    for i2 in range(len(G.batches))]
            if k < 2:
                if not (isinstance(g, int) and g == 0):
                    eng.wait_ge(av_done, G.unit(0))
                return
            p = k - 2
            if ends[p]:
                eng.wait_ge(av_done, G.unit(sum(ends[:p])) + 1)
            else:
                per = sum(not e for e in ends)
                before = sum(not e for e in ends[:p])
                start = g * 8 if G.sb else g * 4 + 16
                eng.wait_ge(at_used, start + (before + 1))

        block = ctx.enter_context(nc.Block())

        @block.sync
        def _(sp):
            sp.dma_start(small[:, :, :], consts.rearrange("p (i c) -> p i c", i=4)).then_inc(s_const, 16)
            sp.dma_start(y[:, 0, :], x_tok[0]).then_inc(s_x[0], 16)

            def load_tile(n, col):
                if not (isinstance(n, int) and n == 0):
                    sp.wait_ge(wt_lo, n)
                sp.dma_start(w_raw[:, :, :], w_in_v[:, :, bass.ds(col, P)]).then_inc(wt_in, 16)

            for t in range(3):
                load_tile(t, SB_W * t)
                if t == 0:
                    for b in range(1, TB):
                        sp.dma_start(y[:, b, :], x_tok[b]).then_inc(s_x[b], 16)
                    sp.dma_start(g_sub, subln_gain.rearrange("a d -> d a")).then_inc(s_lam, 16)
                    for i, v in enumerate((lambda_q1, lambda_k1, lambda_q2, lambda_k2)):
                        sp.dma_start(lams[:, i, :], v.broadcast_to([P, HD])).then_inc(s_lam, 16)
            with sp.Fori(1, SB_GROUPS) as g:
                for t in range(3):
                    load_tile(g * 3 + t, g * P + SB_W * t)
            sp.dma_start(cs[:, :, :], rope).then_inc(s_rope, 16)
            with sp.Fori(0, 4) as g:
                for t in range(3):
                    load_tile(g * 3 + (12 + t), g * P + SB_W * (3 + t))

            def load_branch(i):
                sp.wait_ge(wt_lo, i * 3 + 26)
                sp.dma_start(w_raw[:, 0:4, :], wa_v[:, :, bass.ds(i * P, P)]).then_inc(wt_in, 16)
                sp.dma_start(w_raw[:, 4:8, :], wb_v[:, :, bass.ds(i * P, P)]).then_inc(wt_in, 16)

            load_tile(24, GATE_A)
            load_tile(25, GATE_B)
            with sp.Fori(0, KT - 1) as i:
                load_branch(i)
                load_tile(i * 3 + 27, i * P + (GATE_A + P))
                load_tile(i * 3 + 28, i * P + (GATE_B + P))
            load_branch(KT - 1)

            sp.wait_ge(pj_done, 80)
            for k in range(KT):
                if k >= 2:
                    sp.wait_ge(wo_split, k - 1)
                sp.dma_start(wo_raw[:, k % 2, :], wo_v[k]).then_inc(wo_in[k % 2], 16)
                if k == 1:
                    sp.wait_ge(m_ready, KT)
                    sp.wait_ge(wt_lo, 48)
                    sp.dma_start(gains[:, 0, :], ln1_gain.broadcast_to([P, D])).then_inc(s_gain1, 16)
                    sp.dma_start(gains[:, 1, :], ln1_bias.broadcast_to([P, D])).then_inc(s_gain1, 16)
                    for s in range(2):
                        sp.dma_start(rows[s][:, :], x_tok[s]).then_inc(row_in[s], 16)
            with sp.Fori(0, 3) as j:
                for s in range(2):
                    sp.wait_ge(x1_turned, j * 4 + (2 * s + 2))
                    sp.wait_ge(x1_kept, j * 2 + (s + 1))
                    sp.dma_start(rows[s][:, :], x_tok[j * 2 + (2 + s)]).then_inc(row_in[s], 16)

            def load_up(c, t, first=False):
                if not first:
                    sp.wait_ge(w1_lo, c * 2 + (t - 1))
                sp.dma_start(w1_raw[t][:, :, :], w1_v[:, :, bass.ds(c * 2 * P + t * P, P)]).then_inc(w1_in[t], 16)

            def load_down(c, t, first=False):
                if not first:
                    sp.wait_ge(w2_lo, c * 2 + (t - 1))
                sp.dma_start(w2_raw[t][:, :], w2_v[c * 2 + t]).then_inc(w2_in[t], 16)

            sp.wait_ge(wo_split, KT)
            for t in range(2):
                load_up(0, t, True)
            sp.wait_ge(mt_lo, TB)
            sp.wait_ge(o_done, 2 * TB)
            for t in range(2):
                load_down(0, t, True)
            sp.wait_ge(x1_ready, TB)
            sp.dma_start(gains[:, 0, :], ln2_gain.broadcast_to([P, D])).then_inc(s_gain2, 16)
            sp.dma_start(gains[:, 1, :], ln2_bias.broadcast_to([P, D])).then_inc(s_gain2, 16)
            with sp.Fori(1, FC) as c:
                for t in range(2):
                    load_up(c, t)
                for t in range(2):
                    load_down(c, t)
            with sp.Fori(0, TB // 2) as j:
                for s in range(2):
                    sp.wait_ge(f_ready, j * 2 + (s + 1))
                    sp.dma_start(out_tok[j * 2 + s], rows[s][:, :]).then_inc(s_out[s], 16)
            for s in range(2):
                sp.wait_ge(s_out[s], 16 * (TB // 2))

        @block.tensor
        def _(pe):
            def half_matmuls(n_slot, h, last):
                o = p_proj[:, h, :]
                for k in range(KT):
                    cols = slice(h * NH, h * NH + NH)
                    pe.matmul(o, w_hi[n_slot][:, k, :], xt_h[:, k, cols], start=(k == 0), stop=False)
                    yield
                    pe.matmul(o, w_hi[n_slot][:, k, :], xt_l[:, k, cols], start=False, stop=False)
                    yield
                    mm = pe.matmul(o, w_lo[n_slot][:, k, :], xt_h[:, k, cols], start=False, stop=(k == KT - 1))
                    if k == KT - 1:
                        last(mm)
                    yield

            def filler(G):
                for t in range(G.tiles):
                    n = G.tile(t)
                    for h in range(2):
                        if h == 0:
                            pe.wait_ge(wt_lo, n + 1)
                        if t == 0:
                            pe.wait_ge(pj_plain, G.g * 6 + (5 + h) if G.sb else G.g * 2 + (17 + h))
                        elif G.rope:
                            pe.wait_ge(rp_free, G.roped(t - 1, h) + 1)
                        else:
                            pe.wait_ge(pj_plain, G.plain(t - 1, h) + 1)
                        yield from half_matmuls(t, h, lambda mm: mm.then_inc(pj_done, 1))

            def scores(g, j):
                m, qb = j % 2, j // 2
                width = (qb + 1) * P
                z = p_z[j % 2]
                if not (isinstance(g, int) and g == 0 and j < 2):
                    pe.wait_ge(z_read, g * 16 + (j - 1))
                lhs = q_st[m][:, qb * P:(qb + 1) * P]
                for lo in range(0, width, NH):
                    w = max(min(width - lo, NH), 256)
                    pe.matmul(z[:, lo:lo + w], lhs, k_hi[m][:, lo:lo + w], start=True, stop=False)
                    mm = pe.matmul(z[:, lo:lo + w], lhs, k_lo[m][:, lo:lo + w], start=False, stop=True)
                mm.then_inc(qk_done, 1)

            def first_scores(g):
                pe.wait_ge(st_act, g * 4 + 4)
                pe.wait_ge(st_dve, g * 4 + 4)
                pe.wait_ge(st_pool, g * 2 + 2)
                scores(g, 0)
                scores(g, 1)

            def attention(G):
                g = G.g
                fill = filler(G)
                done = [0]

                def fill_to(n):
                    while done[0] < n:
                        next(fill)
                        done[0] += 1
                    if n == 48 * G.tiles:
                        for _ in fill:
                            raise AssertionError

                fill_to(12)
                scores(g, 2)
                fill_to(24)
                if not G.sb:
                    scores(g, 3)
                pe.wait_ge(pj_plain, g * 6 + 6 if G.sb else g * 2 + 18)
                for vb in range(2):
                    if not (isinstance(g, int) and g == 0 and vb == 0):
                        pe.wait_ge(tr_read, G.tr(vb))
                    for i in range(4):
                        blk = 4 * vb + i
                        mm = pe.transpose(p_tr[:, i * P:(i + 1) * P], stage[2][:, blk * P:(blk + 1) * P], ident)
                    mm.then_inc(tr_done, 1)
                    if vb == 0:
                        fill_to(G.head - 6)

                def turn(k):
                    u, b = G.batches[k]
                    qb = u // 2 if G.sb else u
                    if b == 0:
                        wait_weights(pe, G, u)
                    pe.wait_ge(tr_read, G.tr(k + 2))
                    first_blk, n, _ = span(qb, b)
                    for i in range(n):
                        blk = first_blk + i
                        w = sb_be[u % 4] if G.sb else df_e1[u % 3]
                        mm = pe.transpose(p_tr[:, i * P:(i + 1) * P], w[:, blk * P:(blk + 1) * P], ident)
                    mm.then_inc(tr_done, 1)

                def values(k):
                    u, b = G.batches[k]
                    qb = u // 2 if G.sb else u
                    first_blk, n, end = span(qb, b)
                    pe.wait_ge(tr_read, G.tr(k + 2) + 1)
                    if b == 0 and not (isinstance(g, int) and g == 0 and u == 0):
                        pe.wait_ge(av_read, G.unit(u))
                    for i in range(n):
                        blk = first_blk + i
                        if G.sb:
                            mm = pe.matmul(p_av[:, 0:256], v_st[:, blk, u % 2, :], a_t[:, k % 2, i, :, :],
                                           start=(blk == 0), stop=(blk == qb))
                        else:
                            mm = pe.matmul(p_av[:, 0:P], v_f[:, blk, :], w_t[:, k % 2, i * P:(i + 1) * P],
                                           start=(blk == 0), stop=(blk == qb))
                    mm.then_inc(av_done if end else at_used, 1)

                fill_to(G.head)
                for k, (u, b) in enumerate(G.batches):
                    last_b = k + 1 == len(G.batches) or G.batches[k + 1][0] != u
                    turn(k)
                    if k:
                        values(k - 1)
                    if G.sb:
                        if b == 0 and u + 3 < G.nunits:
                            scores(g, u + 3)
                    elif u + 2 < G.nunits:
                        if b == 0:
                            scores(g, 2 * u + 4)
                        if last_b:
                            scores(g, 2 * u + 5)
                    fill_to(G.until[k])
                if not (isinstance(g, int) and g == GROUPS - 1):
                    first_scores(g + 1)
                values(len(G.batches) - 1)

            pe.wait_ge(s_const, 16)
            for n in range(2 * TB):
                tb, j = n // 2, n % 2
                if j == 0:
                    pe.wait_ge(s_x[tb], 16)
                if n >= 8:
                    pe.wait_ge(xt_lo, n - 7)
                for i in range(4):
                    mm = pe.transpose(x_banks[n % 8][:, i * P:(i + 1) * P],
                                      y[:, tb, (4 * j + i) * P:(4 * j + i + 1) * P], ident)
                mm.then_inc(xt_turned, 1)
            for t in range(3):
                for h in range(2):
                    if h == 0:
                        pe.wait_ge(wt_lo, t + 1)
                    pe.wait_ge(xt_lo, 2 * TB)
                    if t > 0:
                        pe.wait_ge(pj_plain, 2 * (t - 1) + h + 1)
                    for _ in half_matmuls(t, h, lambda mm: mm.then_inc(pj_done, 1)):
                        pass
            pe.wait_ge(s_zero, 4)
            first_scores(0)
            attention(Group(0, True, 3, False))
            with pe.Fori(1, SB_GROUPS - 1) as g:
                attention(Group(g, True, 3, False))
            attention(Group(SB_GROUPS - 1, True, 3, True))
            attention(Group(SB_GROUPS, False, 3, True))
            with pe.Fori(SB_GROUPS + 1, GROUPS - 1) as g:
                attention(Group(g, False, 3, True))
            attention(Group(GROUPS - 1, False, 2, False))

            pe.wait_ge(tr_read, 160)
            pe.wait_ge(s_one, 1)
            for h in range(4):
                pe.wait_ge(sq_ready, h + 1)
                sq = (be + om)[h]
                for b in range(TB):
                    mm = pe.matmul(p_tr[:, 8 * h + b:8 * h + b + 1], sq[:, b * P:(b + 1) * P], one,
                                   start=True, stop=True)
            mm.then_inc(ss_done, 1)

            def branch(i, first, part):
                if part == 0:
                    pe.wait_ge(wt_lo, i * 3 + 27)
                for h in range(2):
                    if first:
                        pe.wait_ge(z_read, 128)
                    else:
                        pe.wait_ge(br_read, i * 2 + (part - 1))
                    o = p_z[part][:, h * NH:(h + 1) * NH]
                    for k in range(4 * part, 4 * part + 4):
                        cols = slice(h * NH, h * NH + NH)
                        pe.matmul(o, w_hi[2][:, k, :], y_h[:, k, cols], start=(k % 4 == 0), stop=False)
                        pe.matmul(o, w_hi[2][:, k, :], y_l[:, k, cols], start=False, stop=False)
                        mm = pe.matmul(o, w_lo[2][:, k, :], y_h[:, k, cols], start=False, stop=(k % 4 == 3))
                mm.then_inc(br_done, 1)

            def gates(i):
                for t in range(2):
                    for h in range(2):
                        if h == 0:
                            pe.wait_ge(wt_lo, i * 3 + (28 + t))
                        pe.wait_ge(pj_plain, i * 4 + (35 + 2 * t + h))
                        for _ in half_matmuls(t, h, lambda mm: mm.then_inc(pj_done, 1)):
                            pass

            pe.wait_ge(ya_split, 4)
            branch(0, True, 0)
            for h in range(4):
                for j in range(2):
                    n = 2 * h + j
                    if n == 0:
                        pe.wait_ge(rs_ready, 1)
                        pe.wait_ge(pj_plain, 36)
                    if n >= 2:
                        pe.wait_ge(yn_ready, n - 1)
                    for i in range(4):
                        b = 4 * j + i
                        mm = pe.matmul(p_proj[:, j, i * P:(i + 1) * P],
                                       rs[:, 8 * h + b:8 * h + b + 1].broadcast_to([P, P]), ident,
                                       start=True, stop=True)
                    mm.then_inc(bc_done, 1)
            pe.wait_ge(yb_split, 4)
            branch(0, True, 1)
            pe.wait_ge(yn_ready, 8)
            gates(0)
            with pe.Fori(1, KT - 1) as i:
                branch(i, False, 0)
                branch(i, False, 1)
                gates(i)
            branch(KT - 1, False, 0)
            branch(KT - 1, False, 1)

            def project_out(tb, s, first):
                pe.wait_ge(mt_lo, tb + 1)
                if first:
                    pe.wait_ge(br_read, 2 * KT)
                elif not isinstance(tb, int):
                    pe.wait_ge(o_read, tb * 2 - 2)
                for h in range(2):
                    o = p_z[s][:, h * NH:(h + 1) * NH]
                    for k in range(KT):
                        if first:
                            pe.wait_ge(wo_split, k + 1)
                        cols = slice(h * NH, h * NH + NH)
                        pe.matmul(o, m_h[s][:, k, :], wo_h[:, k, cols], start=(k == 0), stop=False)
                        pe.matmul(o, m_h[s][:, k, :], wo_l[:, k, cols], start=False, stop=False)
                        mm = pe.matmul(o, m_l[s][:, k, :], wo_h[:, k, cols], start=False, stop=(k == KT - 1))
                    mm.then_inc(o_done, 1)

            def turn_x1(tb, s):
                pe.wait_ge(x1_ready, tb + 1)
                for j in range(2):
                    if not (isinstance(tb, int) and tb == 0):
                        pe.wait_ge(x1_lo, tb * 2 + (j - 1))
                    for i in range(4):
                        blk = 4 * j + i
                        mm = pe.transpose(p_proj[:, j, i * P:(i + 1) * P], rows[s][:, blk * P:(blk + 1) * P], ident)
                    mm.then_inc(x1_turned, 1)

            project_out(0, 0, True)
            project_out(1, 1, False)
            turn_x1(0, 0)
            with pe.Fori(1, TB // 2) as j:
                project_out(j * 2, 0, False)
                turn_x1(j * 2 - 1, 1)
                project_out(j * 2 + 1, 1, False)
                turn_x1(j * 2, 0)

            def up(c, par, first=False):
                for h in range(2):
                    if first and h == 1:
                        turn_x1(TB - 1, 1)
                        pe.wait_ge(x1_lo, 2 * TB)
                    for t in range(2):
                        bank = 2 * h + t
                        if h == 0:
                            pe.wait_ge(w1_lo, c * 2 + (t + 1))
                        if first:
                            if t == 0 and h == 0:
                                pe.wait_ge(x1_lo, 8)
                            o = dn_banks[bank]
                        else:
                            o = up_banks[bank]
                            if isinstance(c, int) and c == 1:
                                pass
                            else:
                                pe.wait_ge(h_ready, c * 4 + (bank - 3))
                        for k in range(KT):
                            cols = slice(h * NH, h * NH + NH)
                            pe.matmul(o, w1_h[t][:, k, :], xt_h[:, k, cols], start=(k == 0), stop=False)
                            pe.matmul(o, w1_h[t][:, k, :], xt_l[:, k, cols], start=False, stop=False)
                            mm = pe.matmul(o, w1_l[t][:, k, :], xt_h[:, k, cols], start=False, stop=(k == KT - 1))
                        mm.then_inc(up_done, 1)

            def down(c, par):
                for t in range(2):
                    pe.wait_ge(w2_lo, c * 2 + (t + 1))
                pe.wait_ge(h_lo, c * 4 + 4)
                for tb in range(TB):
                    for h in range(2):
                        n = 2 * tb + h
                        if isinstance(c, int) and c == 0 and n < 4:
                            pe.wait_ge(h_ready, 4)
                        else:
                            pe.wait_ge(dn_added, c * 16 + (n - 3))
                        o = dn_banks[n % 4]
                        for t in range(2):
                            rws = slice(tb * P, tb * P + P)
                            cols = slice(h * NH, h * NH + NH)
                            pe.matmul(o, h_h[par][t][:, rws], w2_h[t][:, cols], start=(t == 0), stop=False)
                            pe.matmul(o, h_h[par][t][:, rws], w2_l[t][:, cols], start=False, stop=False)
                            mm = pe.matmul(o, h_l[par][t][:, rws], w2_h[t][:, cols], start=False, stop=(t == 1))
                        mm.then_inc(dn_done, 1)

            pe.wait_ge(o_read, 2 * TB)
            up(0, 0, True)
            up(1, 1)
            down(0, 0)
            with pe.Fori(1, FC // 2) as j:
                up(j * 2, 0)
                down(j * 2 - 1, 1)
                up(j * 2 + 1, 1)
                down(j * 2, 0)
            down(FC - 1, 1)

        @block.scalar
        def _(act):
            act.wait_ge(lam_dots, 1)
            act.activation(exps, dots, ACT.Exp).then_inc(lam_exps, 1)
            for n in range(2 * TB):
                tb, j = n // 2, n % 2
                act.wait_ge(xt_turned, n + 1)
                act.activation(xt_h[:, 4 * j:4 * j + 4, tb * P:(tb + 1) * P], by_block(x_banks[n % 8]),
                               ACT.Copy).then_inc(xt_hi, 1)

            def plain(n, h, dst, wait_dst):
                act.wait_ge(pj_done, n * 2 + (h + 1))
                wait_dst()
                act.activation(dst[:, h * NH:(h + 1) * NH], p_proj[:, h, :], ACT.Copy).then_inc(pj_plain, 1)

            for t in range(3):
                for h in range(2):
                    plain(t, h, stage[t], lambda: None)

            def stacks(g, roped, part):
                if part == 0:
                    wait_stage(act, g, roped)
                    for m in range(2):
                        r = slice(HD * m, HD * m + HD)
                        act.activation(q_st[m][r, :], stage[0][r, :], ACT.Copy).then_inc(st_act, 1)
                if part > 0:
                    m = part - 1
                    r, o = slice(HD * m, HD * m + HD), slice(HD * (1 - m), HD * (1 - m) + HD)
                    act.activation(k_hi[m][o, :], stage[1][r, :], ACT.Copy).then_inc(st_act, 1)

            def attention(G):
                g = G.g

                def project_done(k):
                    for i in ([0] if k < 0 else G.halves_at(k)):
                        t, h = i // 2, i % 2
                        if G.is_rope(t):
                            act.wait_ge(pj_done, G.tile(t) * 2 + (h + 1))
                            if not (isinstance(g, int) and g == SB_GROUPS - 1 and i == 0):
                                act.wait_ge(rp_done, G.roped(t, h))
                            for qd in range(4):
                                mm = act.activation(swap[32 * qd:32 * qd + 32, :],
                                                    p_proj[32 * (qd ^ 1):32 * (qd ^ 1) + 32, h, :], ACT.Copy)
                            mm.then_inc(rp_swap, 1)
                        else:
                            def free():
                                if t == 2:
                                    act.wait_ge(tr_done, G.tr(2))
                                else:
                                    act.wait_ge(st_act, g * 4 + 4)
                                    act.wait_ge(st_dve, g * 4 + 4)
                                    act.wait_ge(st_pool, g * 2 + 2)
                            plain(G.tile(t), h, stage[t], free)

                def weights_om(u):
                    qb = u // 2
                    act.wait_ge(qk_done, G.z(u) + 1)
                    if u < 4:
                        if not (isinstance(g, int) and g == 0) and u == 0:
                            act.wait_ge(tr_done, G.tr(0))
                    else:
                        wait_weights(act, G, u - 4)
                    act.activation(sb_om[u % 4][:, 0:(qb + 1) * P], p_z[u % 2][:, 0:(qb + 1) * P], ACT.Sigmoid,
                                   scale=-SCALE).then_inc(om_ready, 1)

                def weights_be(u):
                    qb = u // 2
                    if u >= 4:
                        last = max(k for k, x in enumerate(G.batches) if x[0] == u - 4)
                        act.wait_ge(tr_done, G.tr(last + 2) + 1)
                    act.activation(sb_be[u % 4][:, 0:(qb + 1) * P], p_z[u % 2][:, 0:(qb + 1) * P], ACT.Sigmoid,
                                   scale=SCALE).then_inc(z_read, 1)

                def exponentials(u, m):
                    act.wait_ge(pk_ready, G.z(2 * u + m) - 63)
                    if m == 0:
                        if u >= 3:
                            last = max(k for k, x in enumerate(G.batches) if x[0] == u - 3)
                            act.wait_ge(tr_done, G.tr(last + 2) + 1)
                        else:
                            act.wait_ge(tr_done, G.tr(0))
                            if u == 2:
                                act.wait_ge(av_done, G.unit(0))
                    act.activation((df_e1, df_e2)[m][u % 3][:, 0:(u + 1) * P], p_z[m][:, 0:(u + 1) * P], ACT.Exp,
                                   bias=n_peak[u % 2][:, m:m + 1], scale=SCALE,
                                   accum_out=e_sum[u % 2][:, m:m + 1]).then_inc(z_read, 1)

                def out_up(u):
                    if not G.sb:
                        apart(act)
                    act.wait_ge(av_done, G.unit(u) + 1)
                    if G.sb:
                        if not (isinstance(g, int) and g == 0 and u == 0):
                            act.wait_ge(av_read, G.unit(u))
                        act.activation(y_up[0:HD, :], p_av[HD:P, 0:256], ACT.Copy).then_inc(av_up, 1)
                    else:
                        act.activation(y[:, g, u * P:(u + 1) * P] if isinstance(g, int) else
                                       y[:, bass.ds(g, 1), u * P:(u + 1) * P].rearrange("p a c -> p (a c)"),
                                       p_av[:, 0:P], ACT.Copy).then_inc(av_read, 1)

                for u in range(3 if G.sb else 2):
                    if G.sb:
                        weights_om(u)
                        weights_be(u)
                    else:
                        exponentials(u, 0)
                        exponentials(u, 1)
                for vb in range(2):
                    act.wait_ge(tr_done, G.tr(vb) + 1)
                    if not (isinstance(g, int) and g == 0) and vb == 0:
                        act.wait_ge(av_done, G.unit(0))
                    if G.sb:
                        act.activation(v_st[:, 4 * vb:4 * vb + 4, :, 0:HD],
                                       p_tr[:, :].rearrange("p (b m d) -> p b m d", b=4, m=2),
                                       ACT.Copy).then_inc(tr_hi, 1)
                    else:
                        act.activation(v_f[:, 4 * vb:4 * vb + 4, :], by_block(p_tr[:, :]), ACT.Copy)\
                           .then_inc(tr_read, 1)
                project_done(-1)
                for k, (u, b) in enumerate(G.batches):
                    qb = u // 2 if G.sb else u
                    _, n, last_b = span(qb, b)
                    act.wait_ge(tr_done, G.tr(k + 2) + 1)
                    at_free(act, G, k)
                    if G.sb:
                        act.activation(a_t[:, k % 2, 0:n, 0, :], by_block(p_tr[:, 0:n * P], n), ACT.Copy)\
                           .then_inc(tr_hi, 1)
                    else:
                        act.activation(w_t[:, k % 2, 0:n * P], p_tr[:, 0:n * P], ACT.Copy).then_inc(tr_read, 1)
                    if b == 0 and u > 0:
                        out_up(u - 1)
                    if G.sb:
                        if b == 0 and u + 3 < G.nunits:
                            weights_om(u + 3)
                        if last_b and u + 3 < G.nunits:
                            weights_be(u + 3)
                    elif u + 2 < G.nunits:
                        if b == 0:
                            exponentials(u + 2, 0)
                        if last_b:
                            exponentials(u + 2, 1)
                    if stack_part(G, k) is not None:
                        stacks(g + 1, G.rope, stack_part(G, k))
                    project_done(k)
                out_up(G.nunits - 1)

            for part in range(3):
                stacks(0, False, part)
            attention(Group(0, True, 3, False))
            with act.Fori(1, SB_GROUPS - 1) as g:
                attention(Group(g, True, 3, False))
            attention(Group(SB_GROUPS - 1, True, 3, True))
            attention(Group(SB_GROUPS, False, 3, True))
            with act.Fori(SB_GROUPS + 1, GROUPS - 1) as g:
                attention(Group(g, False, 3, True))
            attention(Group(GROUPS - 1, False, 2, False))

            act.wait_ge(av_read, 96)
            act.wait_ge(tr_done, 160)
            for h in range(4):
                act.activation((be + om)[h][:, :], y[:, 4 + h, :], ACT.Square).then_inc(sq_ready, 1)
            act.wait_ge(v_eps, 1)
            act.activation(rs_t, rs_v, ACT.Sqrt).then_inc(v_root, 1)
            for h in range(4):
                act.wait_ge(yn_ready, 2 * h + 2)
                act.activation(y_h[:, 4 + h, :], y[:, 4 + h, :], ACT.Copy).then_inc(yb_hi, 1)
            for t in range(2):
                act.wait_ge(pj_plain, 34 + 2 * t)
                act.activation(stage[t][:, :], stage[t][:, :], ACT.Sigmoid).then_inc(gate_ready, 1)

            def gates(i):
                for t in range(2):
                    for h in range(2):
                        act.wait_ge(pj_done, i * 4 + (53 + 2 * t + h))
                        if h == 0:
                            act.wait_ge(m_ready, i + 1)
                        act.activation(stage[t][:, h * NH:(h + 1) * NH], p_proj[:, h, :], ACT.Sigmoid)\
                           .then_inc(pj_plain, 1)

            with act.Fori(0, KT - 1) as i:
                gates(i)

            def split_merged(tb, s, first):
                if first:
                    if s == 0:
                        act.wait_ge(br_done, 2 * KT)
                        act.wait_ge(m_ready, KT)
                else:
                    apart(act)
                    act.wait_ge(o_done, tb * 2 - 2)
                act.activation(m_h[s][:, :, :], res_rows(tb), ACT.Copy).then_inc(mt_hi, 1)

            def norm(tb, s):
                act.wait_ge(ln_var, tb + 1)
                act.activation(ln_s[s], ln_v[s], ACT.Sqrt).then_inc(ln_root, 1)

            def keep(tb, s):
                apart(act)
                act.wait_ge(x1_ready, tb + 1)
                act.wait_ge(mt_lo, tb + 1)
                act.activation(res_rows(tb), by_block(rows[s][:, :], 8), ACT.Copy, scale=ALPHA)\
                   .then_inc(x1_kept, 1)
                for j in range(2):
                    apart(act)
                    act.wait_ge(x1_turned, tb * 2 + (j + 1))
                    act.activation(xt_h[:, 4 * j:4 * j + 4, bass.ds(tb * P, P)], by_block(p_proj[:, j, :]),
                                   ACT.Copy).then_inc(x1_hi, 1)

            split_merged(0, 0, True)
            split_merged(1, 1, True)
            norm(0, 0)
            keep(0, 0)
            with act.Fori(1, TB // 2) as j:
                split_merged(j * 2, 0, False)
                norm(j * 2 - 1, 1)
                keep(j * 2 - 1, 1)
                split_merged(j * 2 + 1, 1, False)
                norm(j * 2, 0)
                keep(j * 2, 0)
            norm(TB - 1, 1)

            def hidden(c, par, first=False, keep_last=False):
                for n in range(4):
                    h, t = n // 2, n % 2
                    if first and n == 2:
                        keep(TB - 1, 1)
                    o = (dn_banks if first else up_banks)[n]
                    act.wait_ge(up_done, c * 4 + (n + 1))
                    if not (first and n < 2):
                        act.wait_ge(h_ready, c * 4 + (n - 1))
                    act.activation(relu[:, n % 2, :], o, ACT.Relu).then_inc(up_relu, 1)
                    act.wait_ge(h_ready, c * 4 + (n + 1))
                    if not (isinstance(c, int) and c < 2) and n == 0:
                        act.wait_ge(dn_done, c * 16 - 16)
                    act.activation(h_h[par][t][:, h * NH:(h + 1) * NH], h_f[:, n % 2, :], ACT.Copy)\
                       .then_inc(h_hi, 1)

            hidden(0, 0, True)
            hidden(1, 1)
            with act.Fori(1, FC // 2) as j:
                hidden(j * 2, 0)
                hidden(j * 2 + 1, 1)
            with act.Fori(0, TB // 2) as j:
                for s in range(2):
                    norm(j * 2 + (TB + s), s)

        @block.vector
        def _(dve):
            own = Chain(dve, dve_own)

            def sub(o, a, b):
                return dve.tensor_tensor(o, a, b.bitcast(F32), ALU.subtract)

            dve.memset(one, 1.0).then_inc(s_one, 1)
            dve.wait_ge(s_lam, 5 * 16)
            own(dve.tensor_tensor(lams[:, 0, :], lams[:, 0, :], lams[:, 1, :], ALU.mult))
            own.link(dve.tensor_tensor(lams[:, 2, :], lams[:, 2, :], lams[:, 3, :], ALU.mult))
            dve.tensor_reduce(dots, lams[:, 0::2, :], AX_X, ALU.add).then_inc(lam_dots, 1)
            own.link(dve.tensor_scalar(g_sub, g_sub, 1.0 - LAM_INIT, None, ALU.mult))

            def split_tile(slot, arrived):
                dve.wait_ge(wt_in, arrived)
                dve.tensor_copy(w_hi[slot][:, :, :], w_raw[:, :, :]).then_inc(wt_hi, 1)

            for n in range(2 * TB):
                tb, j = n // 2, n % 2
                dve.wait_ge(xt_hi, n + 1)
                o = xt_l[:, 4 * j:4 * j + 4, tb * P:(tb + 1) * P]
                sub(o, by_block(x_banks[n % 8]), xt_h[:, 4 * j:4 * j + 4, tb * P:(tb + 1) * P]).then_inc(xt_lo, 1)
                if n == 0:
                    split_tile(0, 16)
                if n == 8:
                    split_tile(1, 32)
            dve.wait_ge(lam_exps, 1)
            own.link(dve.tensor_scalar(n_lam, exps[:, 1:2], -LAM_INIT, None, ALU.add))
            own.link(dve.tensor_tensor(n_lam, n_lam, exps[:, 0:1], ALU.subtract))
            split_tile(2, 48)
            dve.wait_ge(pj_done, 2)
            split_tile(0, 64)
            dve.wait_ge(pj_done, 4)
            split_tile(1, 80)

            def stacks(g, roped, part):
                rr = [slice(HD * m, HD * m + HD) for m in range(2)]
                if part == 0:
                    wait_stage(dve, g, roped)
                    for m in range(2):
                        dve.tensor_copy(k_hi[m][rr[m], :], stage[1][rr[m], :]).then_inc(st_dve, 1)
                if part > 0:
                    m = part - 1
                    dve.wait_ge(st_act, g * 4 + (m + 1))
                    sub(q_st[m][rr[1 - m], :], stage[0][rr[m], :], q_st[m][rr[m], :]).then_inc(st_dve, 1)

            def attention(G):
                g = G.g

                def split_next(t):
                    n = G.tile(t)
                    dve.wait_ge(pj_done, n * 2 + 2)
                    last = isinstance(g, int) and g == GROUPS - 1
                    split_tile(t, n * 16 + (16 * 4 + (16 if last else 0)))

                def rope_half(t, h):
                    cols = slice(h * NH, h * NH + NH)
                    dve.wait_ge(rp_swap, G.roped(t, h) + 1)
                    if t == 0 and h == 0:
                        dve.wait_ge(st_act, g * 4 + 4)
                        dve.wait_ge(st_dve, g * 4 + 4)
                        dve.wait_ge(st_pool, g * 2 + 2)
                        dve.wait_ge(s_rope, 16)
                    dve.tensor_tensor(stage[t][:, cols], p_proj[:, h, :], cs[:, 0, cols], ALU.mult)\
                       .then_inc(rp_free, 1)

                def rope_sum(t, h):
                    cols = slice(h * NH, h * NH + NH)
                    dve.wait_ge(rp_sin, G.roped(t, h) + 1)
                    dve.wait_ge(rp_free, G.roped(t, h) + 1)
                    dve.tensor_tensor(stage[t][:, cols], stage[t][:, cols], swap[:, :], ALU.add)\
                       .then_inc(rp_done, 1)

                def scans(u):
                    o, w = sb_om[u % 4], u // 2 * P
                    dg = o[:, w:w + P][:, ::-1]
                    dve.wait_ge(om_ready, G.unit(u) + 1)
                    scan = dve.tensor_tensor_scan(dg, dg, loose[:, ::-1], 1.0, ALU.mult, ALU.max)
                    if w:
                        own.link(scan)
                        rest = o[:, 0:w][:, ::-1]
                        scan = dve.tensor_tensor_scan(rest, rest, rest, o[:, w:w + 1], ALU.mult, ALU.bypass)
                    if u % 2:
                        scan.then_inc(om_odd, 1)
                    else:
                        scan.then_inc(om_even, 1)

                def product(u):
                    o, e, w = sb_om[u % 4], sb_be[u % 4], (u // 2 + 1) * P
                    if u % 2 == 0:
                        dve.wait_ge(om_even, G.g * 8 + (u // 2 + 1))
                        dve.wait_ge(be_masked, G.unit(u) + 1)
                        dve.tensor_tensor(e[:, 0:w - 1], e[:, 0:w - 1], o[:, 1:w], ALU.mult).then_inc(a_even, 1)

                def peaks(u, m):
                    s = u % 2
                    dve.wait_ge(qk_done, G.z(2 * u + m) + 1)
                    z = p_z[m]
                    dg = slice(u * P, (u + 1) * P)
                    own.link(dve.tensor_tensor(z[:, dg], z[:, dg], cap, ALU.min))
                    own.link(dve.tensor_reduce(peak[s][:, m:m + 1], z[:, 0:(u + 1) * P], AX_X, ALU.max))
                    dve.tensor_scalar(n_peak[s][:, m:m + 1], peak[s][:, m:m + 1], -SCALE, None, ALU.mult)\
                       .then_inc(pk_ready, 1)

                def combine(u):
                    s = u % 2
                    w = (u + 1) * P
                    dve.wait_ge(z_read, G.z(2 * u + 1) + 1)
                    own.link(dve.reciprocal(e_inv[s], e_sum[s]))
                    own.link(dve.tensor_tensor(c_neg[s][:, 0:1], e_inv[s][:, 1:2], n_lam, ALU.mult))
                    e1, e2 = df_e1[u % 3], df_e2[u % 3]
                    own.link(dve.tensor_scalar(e2[:, 0:w], e2[:, 0:w], c_neg[s][:, 0:1], None, ALU.mult))
                    dve.scalar_tensor_tensor(out=e1[:, 0:w], in0=e1[:, 0:w], scalar=e_inv[s][:, 0:1],
                                             in1=e2[:, 0:w], op0=ALU.mult, op1=ALU.add).then_inc(a_ready, 1)

                def out_low(u):
                    m, qb = u % 2, u // 2
                    dve.wait_ge(av_up, G.unit(u) + 1)
                    dve.tensor_tensor(y_sum[0:HD, :], p_av[0:HD, 0:256], y_up[0:HD, :], ALU.add)\
                       .then_inc(av_read, 1)

                def out_sum(u):
                    m, qb = u % 2, u // 2
                    dve.wait_ge(av_read, G.unit(u) + 1)
                    dst = (y[HD * m:HD * m + HD, g, qb * P:(qb + 1) * P] if isinstance(g, int) else
                           y[HD * m:HD * m + HD, bass.ds(g, 1), qb * P:(qb + 1) * P].rearrange("p a c -> p (a c)"))
                    dve.tensor_tensor(dst, y_sum[0:HD, 0:P], y_sum[0:HD, P:256], ALU.add).then_inc(y_done, 1)

                if G.sb:
                    for u in range(3):
                        scans(u)
                        if u < 2:
                            product(u)
                    for vb in range(2):
                        dve.wait_ge(tr_hi, g * 26 + (vb + 1))
                        sub(v_st[:, 4 * vb:4 * vb + 4, :, HD:P],
                            p_tr[:, :].rearrange("p (b m d) -> p b m d", b=4, m=2),
                            v_st[:, 4 * vb:4 * vb + 4, :, 0:HD]).then_inc(tr_read, 1)
                else:
                    for u in range(2):
                        for m in range(2):
                            peaks(u, m)
                        combine(u)
                dve.wait_ge(pj_done, g * 6 + 6)
                split_tile(2, g * 48 + (16 * 6 + (16 if isinstance(g, int) and g == GROUPS - 1 else 0)))
                to_sum = []
                if G.is_rope(0):
                    rope_half(0, 0)
                    to_sum.append((0, 0))
                for k, (u, b) in enumerate(G.batches):
                    qb = u // 2 if G.sb else u
                    _, n, last_b = span(qb, b)
                    if G.sb:
                        dve.wait_ge(tr_hi, g * 26 + (k + 3))
                        sub(a_t[:, k % 2, 0:n, 1, :], by_block(p_tr[:, 0:n * P], n), a_t[:, k % 2, 0:n, 0, :])\
                            .then_inc(tr_read, 1)
                        if b == 0 and u > 0:
                            out_low(u - 1)
                        if b == 0 and u + 2 < G.nunits:
                            product(u + 2)
                        if b == 0 and u > 0:
                            out_sum(u - 1)
                        if last_b and u + 3 < G.nunits:
                            scans(u + 3)
                    else:
                        if b == 0 and 0 < u < G.nunits - 1:
                            combine(u + 1)
                        if b == 0 and u + 2 < G.nunits:
                            peaks(u + 2, 0)
                        if last_b and u + 2 < G.nunits:
                            peaks(u + 2, 1)
                    while to_sum:
                        rope_sum(*to_sum.pop())
                    if stack_part(G, k) is not None:
                        stacks(g + 1, G.rope, stack_part(G, k))
                    for i in G.halves_at(k):
                        if G.is_rope(i // 2):
                            rope_half(i // 2, i % 2)
                            to_sum.append((i // 2, i % 2))
                        if i in (1, 3):
                            split_next(i // 2)
                if G.sb:
                    out_low(G.nunits - 1)
                    out_sum(G.nunits - 1)

            for part in range(3):
                stacks(0, False, part)
            attention(Group(0, True, 3, False))
            own.loop(1, SB_GROUPS - 1, 14, lambda g: attention(Group(g, True, 3, False)))
            attention(Group(SB_GROUPS - 1, True, 3, True))
            attention(Group(SB_GROUPS, False, 3, True))
            own.loop(SB_GROUPS + 1, GROUPS - 1, 56, lambda g: attention(Group(g, False, 3, True)))
            attention(Group(GROUPS - 1, False, 2, False))

            dve.wait_ge(y_done, 64)
            dve.wait_ge(qk_done, 128)
            dve.wait_ge(av_done, 96)
            for t in range(4):
                own.link(dve.tensor_copy(y_h[:, t, :], y[:, t, :]))
                sub(y_l[:, t, :], y[:, t, :], y_h[:, t, :]).then_inc(ya_split, 1)
            dve.wait_ge(ss_done, 1)
            dve.tensor_scalar(rs_v, p_tr[:, 0:32], 1.0 / P, EPS, ALU.mult, ALU.add).then_inc(v_eps, 1)
            dve.wait_ge(v_root, 1)
            dve.wait_ge(v_eps, 1)
            own.link(dve.reciprocal(rs, rs_t))
            own.link(dve.tensor_tensor(ss, rs_v, rs, ALU.mult))
            own.link(dve.tensor_tensor(ss, ss, rs, ALU.mult))
            own.link(dve.tensor_scalar(ss, ss, -0.5, 1.5, ALU.mult, ALU.add))
            dve.tensor_tensor(rs, rs, ss, ALU.mult).then_inc(rs_ready, 1)
            for h in range(4):
                for j in range(2):
                    cols = slice(j * NH, j * NH + NH)
                    dve.wait_ge(bc_done, 2 * h + j + 1)
                    dve.wait_ge(sq_ready, h + 1)
                    dve.scalar_tensor_tensor(out=y[:, 4 + h, cols], in0=y[:, 4 + h, cols], scalar=g_sub,
                                             in1=p_proj[:, j, :], op0=ALU.mult, op1=ALU.mult)\
                        .then_inc(yn_ready, 1)
                dve.wait_ge(yb_hi, h + 1)
                sub(y_l[:, 4 + h, :], y[:, 4 + h, :], y_h[:, 4 + h, :]).then_inc(yb_split, 1)

            def merge(i, tiles, branch_next):
                for t in range(2):
                    dve.wait_ge(br_done, i * 2 + (t + 1))
                    if isinstance(i, int) and i == 0:
                        dve.wait_ge(gate_ready, t + 1)
                    else:
                        dve.wait_ge(pj_plain, i * 4 + (32 + 2 * t + 2))
                    dve.tensor_tensor(stage[t][:, :], stage[t][:, :], p_z[t][:, :], ALU.mult).then_inc(br_read, 1)
                dve.wait_ge(br_read, i * 2 + 2)
                dst = res[:, i, :] if isinstance(i, int) else \
                    res[:, bass.ds(i, 1), :].rearrange("p a c -> p (a c)")
                dve.tensor_tensor(dst, stage[0][:, :], stage[1][:, :], ALU.add).then_inc(m_ready, 1)
                if branch_next:
                    split_tile(2, i * 64 + (16 * (26 + 4 + 1)) + 16)
                for t in range(tiles):
                    dve.wait_ge(pj_done, i * 4 + (52 + 2 * t + 2))
                    split_tile(t, i * 64 + (16 * (31 + 2 + t)) + 0)

            merge(0, 2, True)
            with dve.Fori(1, KT - 2) as i:
                merge(i, 2, True)
            merge(KT - 2, 0, True)
            merge(KT - 1, 0, False)

            def merged_low(tb, s):
                dve.wait_ge(mt_hi, tb + 1)
                sub(m_l[s][:, :, :], res_rows(tb), m_h[s][:, :, :]).then_inc(mt_lo, 1)

            def wo_tile(k):
                dve.wait_ge(wo_in[k % 2], 16 * (k // 2 + 1))
                own.link(dve.tensor_copy(wo_h[:, k, :], wo_raw[:, k % 2, :]))
                sub(wo_l[:, k, :], wo_raw[:, k % 2, :], wo_h[:, k, :]).then_inc(wo_split, 1)

            def norm_stats(tb, s, base_n):
                for h in range(2):
                    own(dve.bn_stats(stats[s][:, 6 * h:6 * h + 6], rows[s][:, h * NH:(h + 1) * NH]))
                own.sync()
                dve.memset(ln_t[s], 0.0)
                own.link(dve.bn_aggr(aggr[s], stats[s]))
                dve.tensor_scalar(ln_v[s], aggr[s][:, 1:2], EPS, None, ALU.add).then_inc(ln_var, 1)
                dve.wait_ge(ln_var, tb + (base_n + 1))
                dve.wait_ge(ln_root, tb + (base_n + 1))
                own.link(dve.reciprocal(ln_r[s], ln_s[s]))
                own.link(dve.tensor_tensor(ln_t[s], ln_v[s], ln_r[s], ALU.mult))
                own.link(dve.tensor_tensor(ln_t[s], ln_t[s], ln_r[s], ALU.mult))
                own.link(dve.tensor_scalar(ln_t[s], ln_t[s], -0.5, 1.5, ALU.mult, ALU.add))
                own.link(dve.tensor_tensor(ln_r[s], ln_r[s], ln_t[s], ALU.mult))
                own.link(dve.scalar_tensor_tensor(out=rows[s][:, :], in0=rows[s][:, :], scalar=aggr[s][:, 0:1],
                                                  in1=gains[:, 0, :], op0=ALU.subtract, op1=ALU.mult))
                return dve.scalar_tensor_tensor(out=rows[s][:, :], in0=rows[s][:, :], scalar=ln_r[s],
                                                in1=gains[:, 1, :], op0=ALU.mult, op1=ALU.add)

            def layer_norm1(tb, s, count):
                for h in range(2):
                    dve.wait_ge(o_done, tb * 2 + (h + 1))
                    if h == 0:
                        dve.wait_ge(row_in[s], count)
                    cols = slice(h * NH, h * NH + NH)
                    dve.scalar_tensor_tensor(out=rows[s][:, cols], in0=rows[s][:, cols], scalar=ALPHA,
                                             in1=p_z[s][:, cols], op0=ALU.mult, op1=ALU.add).then_inc(o_read, 1)
                dve.wait_ge(o_read, tb * 2 + 2)
                norm_stats(tb, s, 0).then_inc(x1_ready, 1)

            def x1_low(tb):
                for j in range(2):
                    dve.wait_ge(x1_hi, tb * 2 + (j + 1))
                    cols = bass.ds(tb * P, P)
                    sub(xt_l[:, 4 * j:4 * j + 4, cols], by_block(p_proj[:, j, :]), xt_h[:, 4 * j:4 * j + 4, cols])\
                        .then_inc(x1_lo, 1)

            merged_low(0, 0)
            for k in range(KT):
                wo_tile(k)
            merged_low(1, 1)
            dve.wait_ge(s_gain1, 32)
            layer_norm1(0, 0, 16)
            own.loop(1, TB // 2, 18, lambda j: (
                merged_low(j * 2, 0),
                layer_norm1(j * 2 - 1, 1, j * 16),
                x1_low(j * 2 - 2),
                merged_low(j * 2 + 1, 1),
                layer_norm1(j * 2, 0, j * 16 + 16),
                x1_low(j * 2 - 1)))

            def up_high(c, t, first=False):
                if first:
                    if t == 0:
                        dve.wait_ge(o_done, 2 * TB)
                else:
                    dve.wait_ge(up_done, c * 4)
                dve.wait_ge(w1_in[t], c * 16 + 16)
                dve.tensor_copy(w1_h[t][:, :, :], w1_raw[t][:, :, :]).then_inc(w1_hi, 1)

            def down_high(c, t, first=False):
                if not first:
                    dve.wait_ge(dn_done, c * 16)
                dve.wait_ge(w2_in[t], c * 16 + 16)
                dve.tensor_copy(w2_h[t][:, :], w2_raw[t][:, :]).then_inc(w2_hi, 1)

            def hidden(c, n, first=False):
                o = (dn_banks if first else up_banks)[n]
                dve.wait_ge(up_relu, c * 4 + (n + 1))
                if not (first and n < 2):
                    dve.wait_ge(h_lo, c * 4 + (n - 1))
                dve.scalar_tensor_tensor(out=h_f[:, n % 2, :], in0=o, scalar=0.0, in1=relu[:, n % 2, :],
                                         op0=ALU.max, op1=ALU.mult).then_inc(h_ready, 1)

            def hidden_low(c, par, n):
                h, t = n // 2, n % 2
                dve.wait_ge(h_hi, c * 4 + (n + 1))
                cols = slice(h * NH, h * NH + NH)
                sub(h_l[par][t][:, cols], h_f[:, n % 2, :], h_h[par][t][:, cols]).then_inc(h_lo, 1)

            def features(c, par, first=False):
                for n in range(4):
                    if first and n == 2:
                        x1_low(TB - 1)
                    hidden(c, n, first)
                    hidden_low(c, par, n)

            def add_rows(c, n):
                dve.wait_ge(dn_done, c * 16 + (n + 1))
                o = res[:, 4 * (n % 2):4 * (n % 2) + 4, (n // 2) * P:(n // 2 + 1) * P]
                dve.tensor_tensor(o, by_block(dn_banks[n % 4]), o, ALU.add).then_inc(dn_added, 1)

            up_high(0, 0, True)
            up_high(0, 1, True)
            layer_norm1(TB - 1, 1, 64)
            x1_low(TB - 2)
            dve.wait_ge(x1_kept, TB - 1)
            features(0, 0, True)
            down_high(0, 0, True)
            down_high(0, 1, True)
            for t in range(2):
                up_high(1, t)
            features(1, 1)
            for t in range(2):
                up_high(2, t)
            for n in range(16):
                add_rows(0, n)

            def chunk(c, par, more):
                for t in range(2):
                    down_high(c - 1, t)
                features(c, par)
                if more:
                    for t in range(2):
                        up_high(c + 1, t)
                for n in range(16):
                    add_rows(c - 1, n)

            with dve.Fori(1, FC // 2 - 1) as j:
                chunk(j * 2, 0, True)
                chunk(j * 2 + 1, 1, True)
            chunk(FC - 2, 0, True)
            chunk(FC - 1, 1, False)
            down_high(FC - 1, 0)
            down_high(FC - 1, 1)

            dve.wait_ge(s_gain2, 32)

            def layer_norm2(j, first=False):
                for s in range(2):
                    tb = j * 2 + s
                    if not first:
                        dve.wait_ge(s_out[s], j * 16)
                    for h in range(2):
                        dve.wait_ge(dn_done, tb * 2 + (16 * (FC - 1) + h + 1))
                        cols = slice(h * NH, h * NH + NH)
                        dve.tensor_tensor(by_block(rows[s][:, cols]), by_block(dn_banks[2 * s + h]),
                                          res_half(tb, h), ALU.add).then_inc(dn_added, 1)
                    dve.wait_ge(dn_added, tb * 2 + (16 * (FC - 1) + 2))
                    norm_stats(tb, s, TB).then_inc(f_ready, 1)

            layer_norm2(0, True)
            own.loop(1, TB // 2, 18, layer_norm2)

        @block.gpsimd
        def _(pool):
            for m in range(2):
                r = slice(HD * (1 - m), HD * (1 - m) + HD)
                pool.memset(k_lo[m][r, :].bitcast(F32), 0.0).then_inc(s_zero, 2)

            pool.wait_ge(s_zero, 4)

            def tile_low(n, slot):
                pool.wait_ge(wt_hi, n + 1)
                pool.tensor_tensor(w_lo[slot][:, :, :], w_raw[:, :, :], w_hi[slot][:, :, :].bitcast(F32),
                                   ALU.subtract).then_inc(wt_lo, 1)

            def sines(G, t, h):
                pool.wait_ge(rp_swap, G.roped(t, h) + 1)
                pool.tensor_tensor(swap[:, :], swap[:, :], cs[:, 1, h * NH:(h + 1) * NH], ALU.mult)\
                    .then_inc(rp_sin, 1)

            for t in range(5):
                tile_low(t, t % 3)

            def low_keys(g):
                pool.memset(idle, 0.0).then_inc(pool_idle, 1)
                pool.wait_ge(pool_idle, g + 1)
                for m in range(2):
                    r = slice(HD * m, HD * m + HD)
                    if m:
                        pool.wait_ge(st_pool, g * 2 + 1)
                    pool.wait_ge(st_dve, g * 4 + (m + 1))
                    pool.tensor_tensor(k_lo[m][r, :], stage[1][r, :], k_hi[m][r, :].bitcast(F32), ALU.subtract)\
                        .then_inc(st_pool, 1)
                pool.wait_ge(st_pool, g * 2 + 2)

            def mask(G, u):
                e = sb_be[u % 4][:, u // 2 * P:(u // 2 + 1) * P]
                pool.wait_ge(z_read, G.z(u) + 1)
                pool.tensor_tensor(e, e, strict, ALU.mult).then_inc(be_masked, 1)

            def product(G, u):
                o, e, w = sb_om[u % 4], sb_be[u % 4], (u // 2 + 1) * P
                pool.wait_ge(om_odd, G.g * 8 + (u // 2 + 1))
                pool.wait_ge(be_masked, G.unit(u) + 1)
                pool.tensor_tensor(e[:, 0:w - 1], e[:, 0:w - 1], o[:, 1:w], ALU.mult).then_inc(a_odd, 1)

            def attention(G):
                if G.sb:
                    for u in range(3):
                        mask(G, u)
                        if u == 1:
                            product(G, 1)
                tile_low(G.g * 3 + 5, 2)
                if G.is_rope(0):
                    pool.wait_ge(s_rope, 16)
                    sines(G, 0, 0)
                for k, (u, b) in enumerate(G.batches):
                    if G.sb and (k + 1 == len(G.batches) or G.batches[k + 1][0] != u):
                        if u % 2 and u + 2 < G.nunits:
                            product(G, u + 2)
                        if u + 3 < G.nunits:
                            mask(G, u + 3)
                    if stack_part(G, k) == 0:
                        low_keys(G.g + 1)
                    for i in G.halves_at(k):
                        if G.is_rope(i // 2):
                            sines(G, i // 2, i % 2)
                        if i in (1, 3):
                            tile_low(G.tile(i // 2) + 3, i // 2)

            low_keys(0)
            attention(Group(0, True, 3, False))
            with pool.Fori(1, SB_GROUPS - 1) as g:
                attention(Group(g, True, 3, False))
            attention(Group(SB_GROUPS - 1, True, 3, True))
            attention(Group(SB_GROUPS, False, 3, True))
            with pool.Fori(SB_GROUPS + 1, GROUPS - 1) as g:
                attention(Group(g, False, 3, True))
            attention(Group(GROUPS - 1, False, 2, False))
            with pool.Fori(0, KT - 2) as i:
                tile_low(i * 3 + 29, 2)
                tile_low(i * 3 + 30, 0)
                tile_low(i * 3 + 31, 1)
            tile_low(47, 2)

            def up_low(c, t):
                pool.wait_ge(w1_hi, c * 2 + (t + 1))
                pool.tensor_tensor(w1_l[t][:, :, :], w1_raw[t][:, :, :], w1_h[t][:, :, :].bitcast(F32),
                                   ALU.subtract).then_inc(w1_lo, 1)

            def down_low(c, t):
                pool.wait_ge(w2_hi, c * 2 + (t + 1))
                pool.tensor_tensor(w2_l[t][:, :], w2_raw[t][:, :], w2_h[t][:, :].bitcast(F32),
                                   ALU.subtract).then_inc(w2_lo, 1)

            for step, c in ((up_low, 0), (down_low, 0), (up_low, 1), (up_low, 2)):
                for t in range(2):
                    step(c, t)
            with pool.Fori(2, FC - 1) as c:
                for t in range(2):
                    down_low(c - 1, t)
                for t in range(2):
                    up_low(c + 1, t)
            for c in (FC - 2, FC - 1):
                for t in range(2):
                    down_low(c, t)


_INS = ["x", "w_in", "w_branch_a", "w_branch_b", "w_out", "lambda_q1", "lambda_k1", "lambda_q2",
        "lambda_k2", "subln_gain", "ln1_gain", "ln1_bias", "w_ff1", "w_ff2", "ln2_gain", "ln2_bias"]


def kernel(**inputs):
    import numpy as _np
    import concourse.bacc as _bacc
    from concourse import mybir as _mybir
    from concourse.bass_utils import run_bass_kernel_spmd as _run

    nc = _bacc.Bacc("TRN2", target_bir_lowering=False, num_devices=1)
    arrays = {name: _np.ascontiguousarray(inputs[name]) for name in _INS}
    small, rope = const_arrays()
    arrays["consts"], arrays["rope"] = small, rope
    args = [nc.dram_tensor(name, a.shape, _mybir.dt.from_np(a.dtype), kind="ExternalInput").ap()
            for name, a in arrays.items()]
    args.append(nc.dram_tensor("out", (1, S, D), F32, kind="ExternalOutput").ap())
    layer_kernel(nc, *args)
    r = _run(nc, [arrays], core_ids=[0])
    return r.results[0]["out"]
```

```python
from contextlib import ExitStack

import numpy as np

import concourse.bass as bass
from concourse import mybir

F32 = mybir.dt.float32
F32R = mybir.dt.float32r
ALU = mybir.AluOpType
ACT = mybir.ActivationFunctionType
AX_X = mybir.AxisListType.X

P = 128
D = 1024
S = 1024
HD = 64
KT = D // P
TB = S // P
NH = 512
FF = 4096
SB_GROUPS = 4
GROUPS = 8
SCALE = HD ** -0.5
ALPHA = 2.0 ** 0.25
EPS = 1e-5
LAM_INIT = 0.8 - 0.6
BIG = 3.0e38

SB_W = 512
GATE_A = 6 * SB_W
GATE_B = GATE_A + D

SB_UNITS = 16
DF_UNITS = 8
SB_BATCH = [(u, b) for u in range(SB_UNITS) for b in range((u // 2) // 4 + 1)]
DF_BATCH = [(u, b) for u in range(DF_UNITS) for b in range(u // 4 + 1)]


def const_arrays():
    q = np.arange(P)[:, None]
    k = np.arange(P)[None, :]
    ident = (q == k).astype(np.float32)
    strict = (k < q).astype(np.float32)
    cap = np.where(k <= q, np.float32(BIG), np.float32(-BIG)).astype(np.float32)
    inv = np.float32(10000.0) ** (-np.arange(0, HD, 2, dtype=np.float32) / np.float32(HD))
    ang = np.arange(S, dtype=np.float32)[:, None] * inv[None, :].astype(np.float32)
    cos, sin = np.cos(ang).astype(np.float32).T, np.sin(ang).astype(np.float32).T
    rows_c = np.concatenate([cos] * 4, axis=0)
    rows_s = np.concatenate([-sin, sin, -sin, sin], axis=0)
    small = np.concatenate([ident, strict, 1.0 - strict, cap], axis=1).astype(np.float32)
    return small, np.stack([rows_c, rows_s], axis=1).astype(np.float32)


def span(qb, b):
    total = qb + 1
    if total <= 4:
        return 0, total, True
    half = (total + 1) // 2
    return (0, half, False) if b == 0 else (half, total - half, True)


SB_SHARE = (5.5, 3.5, 4.5)
DF_SHARE = (13, 6.5, 8)


class Group:

    def __init__(self, g, sb, tiles, rope):
        self.g, self.sb, self.tiles, self.rope = g, sb, tiles, rope
        self.last = isinstance(g, int) and g == GROUPS - 1
        self.batches = SB_BATCH if sb else DF_BATCH
        self.nunits = SB_UNITS if sb else DF_UNITS
        total = 48 * tiles
        self.head = 30 if sb else 38
        weight = np.cumsum([self.share(u, b) for u, b in self.batches])
        self.until = [int(self.head + w * (total - self.head) // weight[-1]) for w in weight]

    def share(self, u, b):
        alone = (u, 1) not in self.batches
        if self.sb:
            return SB_SHARE[0 if alone else 1 if b == 0 and u < SB_UNITS - 3 else 2]
        return DF_SHARE[0 if alone else 1 if u < DF_UNITS - 2 else 2]

    def z(self, j):
        return self.g * 16 + j

    def unit(self, u):
        return self.g * 16 + u if self.sb else self.g * 8 + (u + 32)

    def tr(self, k):
        return self.g * 26 + k if self.sb else self.g * 14 + (k + 48)

    def tile(self, t):
        return self.g * 3 + (3 + t)

    def plain(self, t, h):
        if not self.rope:
            if self.last:
                return 32 + 2 * t + h
            return self.g * 6 + (6 + 2 * t + h)
        return self.g * 2 + (24 - 6 + h)

    def roped(self, t, h):
        return self.g * 4 + (2 * t + h - 12)

    def is_rope(self, t):
        return self.rope and t < 2

    def halves_at(self, k):
        lo = 24 if k == 0 else self.until[k - 1]
        hi = self.until[k]
        return [i for i in range(1, 2 * self.tiles) if lo < 24 * (i + 1) <= hi]


class Chain:

    def __init__(self, eng, sem):
        self.eng, self.sem, self.base, self.n = eng, sem, 0, 0

    def __call__(self, ins):
        ins.then_inc(self.sem, 1)
        self.n += 1

    def sync(self):
        self.eng.wait_ge(self.sem, self.base + self.n)

    def link(self, ins):
        self(ins)
        self.sync()

    def loop(self, start, end, per, body):
        before = self.n
        with self.eng.Fori(start, end) as i:
            self.base, self.n = i * per + (before - start * per), 0
            body(i)
            assert self.n == per, f"the loop's body counts {self.n}, not {per}"
        self.base, self.n = 0, before + per * (end - start)


def layer_kernel(nc, x, w_in, w_branch_a, w_branch_b, w_out, lambda_q1, lambda_k1, lambda_q2,
                 lambda_k2, subln_gain, ln1_gain, ln1_bias, w_ff1, w_ff2, ln2_gain, ln2_bias,
                 consts, rope, out):
    with ExitStack() as ctx:
        base = (nc.sbuf_base + 63) // 64 * 64

        def at(name, kib, shape, dt=F32, off=0):
            return nc.alloc_sbuf_tensor_at(name, shape, dt, offset=base + int(kib * 1024) + off)

        def pb(name, shape):
            return ctx.enter_context(nc.psum_tensor(name, shape, F32))

        def sem(name):
            return ctx.enter_context(nc.semaphore(name))

        FC = FF // (2 * P)

        xt_h = at("xt_h", 0, [P, KT, S], F32R)
        xt_l = at("xt_l", 32, [P, KT, S], F32R)
        y = at("y", 64, [P, 8, S])
        y_l = at("y_l", 64, [P, 8, S], F32R)
        y_h = at("y_h", 96, [P, 8, S], F32R)
        q_st = [at(f"q_st{m}", 96 + 4 * m, [P, S], F32R) for m in range(2)]
        k_hi = [at(f"k_hi{m}", 104 + 4 * m, [P, S], F32R) for m in range(2)]
        k_lo = [at(f"k_lo{m}", 112 + 4 * m, [P, S], F32R) for m in range(2)]
        v_st = at("v_st", 120, [P, TB, 2, P], F32R)
        v_f = at("v_f", 120, [P, TB, P])
        stage = [at(f"stage{t}", 192 + 4 * t, [P, S]) for t in range(3)]
        be = [at(f"be{i}", 128 + 4 * i, [P, S]) for i in range(2)]
        om = [at(f"om{i}", 136 + 4 * i, [P, S]) for i in range(2)]
        sb_be = be + [y[:, 6, :], y[:, 7, :]]
        sb_om = om + [y[:, 4, :], y[:, 5, :]]
        df_e1 = be + [at("e1_2", 124, [P, S])]
        df_e2 = om + [at("e2_2", 148, [P, S])]
        squares = [at("square0", 112, [P, S]), at("square1", 116, [P, S]), stage[2], be[0]]
        a_t = at("a_t", 144, [P, 2, 4, 2, P], F32R)
        w_t = at("w_t", 144, [P, 2, NH])
        swap = at("swap", 152, [P, NH])
        y_up = at("y_up", 154, [P, 256])
        y_sum = at("y_sum", 155, [P, 256])
        cs = at("cs", 156, [P, 2, S])
        w_raw = at("w_raw", 164, [P, KT, P])
        w_hi = [at(f"w_hi{s}", 168 + 8 * s, [P, KT, P], F32R) for s in range(3)]
        w_lo = [at(f"w_lo{s}", 172 + 8 * s, [P, KT, P], F32R) for s in range(3)]
        small = at("small", 204, [P, 4, P])
        ident, strict, loose, cap = (small[:, i, :] for i in range(4))
        vecs = at("vecs", 206, [P, 256])
        one, n_lam, g_sub = (vecs[:, i:i + 1] for i in range(3))
        dots, exps = vecs[:, 4:6], vecs[:, 6:8]
        idle = vecs[:, 3:4]
        peak, n_peak, e_sum, e_inv, c_neg = (
            [vecs[:, 8 + 4 * i + 2 * p:10 + 4 * i + 2 * p] for p in range(2)] for i in range(5))
        ss, rs, rs_t, rs_v = (vecs[:, 32 + 32 * i:64 + 32 * i] for i in range(4))
        stats = [vecs[:, 160 + 12 * p:172 + 12 * p] for p in range(2)]
        aggr = [vecs[:, 184 + 2 * p:186 + 2 * p] for p in range(2)]
        ln_v, ln_s, ln_r, ln_t = ([vecs[:, 188 + 4 * i + p:189 + 4 * i + p] for p in range(2)]
                                  for i in range(4))
        lams = at("lams", 154, [P, 4, HD])

        res = at("res", 128, [P, KT, S])
        gains = at("gains", 160, [P, 2, D])
        wo_h = at("wo_h", 0, [P, 2, KT, NH], F32R)
        wo_l = at("wo_l", 32, [P, 2, KT, NH], F32R)
        wo_raw = at("wo_raw", 32, [P, 2, KT, NH])
        x1t_h = at("x1t_h", 64, [P, KT, S], F32R)
        x1t_l = at("x1t_l", 96, [P, KT, S], F32R)
        gate_pairs = [stage[:2], [stage[2], at("gate_b1", 160, [P, S])]]
        m_h = [at(f"m_h{s}", 176 + 8 * s, [P, KT, P], F32R) for s in range(2)]
        m_l = [at(f"m_l{s}", 180 + 8 * s, [P, KT, P], F32R) for s in range(2)]
        rows = [at(f"rows{s}", 192 + 4 * s, [P, D]) for s in range(2)]

        h_h = [[at(f"h_h{c}{t}", 32 + 16 * c + 8 * t, [P, S], F32R) for t in range(2)]
               for c in range(2)]
        h_l = [[at(f"h_l{c}{t}", 36 + 16 * c + 8 * t, [P, S], F32R) for t in range(2)]
               for c in range(2)]
        w1_h = [at(f"w1_h{t}", 0 + 8 * t, [P, KT, P], F32R) for t in range(2)]
        w1_l = [at(f"w1_l{t}", 4 + 8 * t, [P, KT, P], F32R) for t in range(2)]
        w2_h = [at(f"w2_h{t}", 16 + 8 * t, [P, D], F32R) for t in range(2)]
        w2_l = [at(f"w2_l{t}", 20 + 8 * t, [P, D], F32R) for t in range(2)]
        w1_raw = [at(f"w1_raw{t}", 168 + 4 * t, [P, KT, P]) for t in range(2)]
        w2_raw = [at(f"w2_raw{t}", 176 + 4 * t, [P, D]) for t in range(2)]
        rows_out = at("rows_out", 64, [P, TB, D])
        w1_last_h, w1_last_l = (at(f"w1_last_{i}", 192 + 4 * i, [P, KT, P], F32R) for i in range(2))
        w2_last_h = [at(f"w2_last_h{t}", 168 + 4 * t, [P, D], F32R) for t in range(2)]
        w2_last_l = [at(f"w2_last_l{t}", 176 + 4 * t, [P, D], F32R) for t in range(2)]
        relu = at("relu", 184, [P, 2, NH])
        h_f = at("h_f", 188, [P, 2, NH])

        def w1_tiles(c, t):
            if t == 0 and isinstance(c, int) and c == FC - 1:
                return w1_last_h, w1_last_l
            return w1_h[t], w1_l[t]

        p_proj = pb("p_proj", [P, 2, NH])
        p_z = [pb(f"p_z{i}", [P, S]) for i in range(2)]
        p_tr = pb("p_tr", [P, NH])
        p_av = pb("p_av", [P, NH])
        x_banks = [p_z[0][:, 0:NH], p_z[0][:, NH:S],
                   p_z[1][:, 0:NH], p_z[1][:, NH:S], p_tr[:, :], p_av[:, :]]
        up_banks = [p_proj[:, 0, :], p_proj[:, 1, :], p_tr[:, :], p_av[:, :]]
        dn_banks = [p_z[0][:, 0:NH], p_z[0][:, NH:S], p_z[1][:, 0:NH], p_z[1][:, NH:S]]


        def last_bank(n):
            return (dn_banks, up_banks)[n // 4 % 2][n % 4]

        s_const, s_rope, s_lam = sem("s_const"), sem("s_rope"), sem("s_lam")
        s_x = [sem(f"s_x{b}") for b in range(TB)]
        s_one, s_zero = sem("s_one"), sem("s_zero")
        xt_turned, xt_hi, xt_lo = sem("xt_turned"), sem("xt_hi"), sem("xt_lo")
        lam_dots, lam_exps = sem("lam_dots"), sem("lam_exps")
        wt_in, wt_hi, wt_lo = sem("wt_in"), sem("wt_hi"), sem("wt_lo")
        pj_done, pj_plain = sem("pj_done"), sem("pj_plain")
        rp_swap, rp_free, rp_sin, rp_done = sem("rp_swap"), sem("rp_free"), sem("rp_sin"), sem("rp_done")
        st_act, st_dve, st_pool = sem("st_act"), sem("st_dve"), sem("st_pool")
        pool_idle = sem("pool_idle")
        qk_done, om_ready, z_read = sem("qk_done"), sem("om_ready"), sem("z_read")
        be_masked, om_even, om_odd, a_even, a_odd = sem("be_masked"), sem("om_even"), sem("om_odd"), sem("a_even"), sem("a_odd")
        pk_ready, a_ready = sem("pk_ready"), sem("a_ready")
        tr_done, tr_hi, tr_read = sem("tr_done"), sem("tr_hi"), sem("tr_read")
        at_used, av_done, av_up, av_read, y_done = (
            sem("at_used"), sem("av_done"), sem("av_up"), sem("av_read"), sem("y_done"))
        sq_ready, ss_done, v_eps, v_root, rs_ready = (
            sem("sq_ready"), sem("ss_done"), sem("v_eps"), sem("v_root"), sem("rs_ready"))
        bc_done, yn_ready = sem("bc_done"), sem("yn_ready")
        ya_split, yb_hi, yb_split = sem("ya_split"), sem("yb_hi"), sem("yb_split")
        gate_ready, br_done, br_read, m_ready = (
            sem("gate_ready"), sem("br_done"), sem("br_read"), sem("m_ready"))
        s_gain1, s_gain2 = sem("s_gain1"), sem("s_gain2")
        wo_in = [sem(f"wo_in{k}") for k in range(KT)]
        wo_hi, wo_even, wo_odd = sem("wo_hi"), sem("wo_even"), sem("wo_odd")
        mt_first_hi, mt_first_lo = sem("mt_first_hi"), sem("mt_first_lo")
        mt_hi, mt_lo, o_done, o_read = sem("mt_hi"), sem("mt_lo"), sem("o_done"), sem("o_read")
        row_in = [sem("row_in0"), sem("row_in1")]
        ln_var, ln_root, x1_ready, x1_kept = sem("ln_var"), sem("ln_root"), sem("x1_ready"), sem("x1_kept")
        x1_turned, x1_hi, x1_lo = sem("x1_turned"), sem("x1_hi"), sem("x1_lo")
        w1_in = [sem("w1_in0"), sem("w1_in1")]
        w2_in = [sem("w2_in0"), sem("w2_in1")]
        w1_hi, w1_lo, w2_hi, w2_lo = sem("w1_hi"), sem("w1_lo"), sem("w2_hi"), sem("w2_lo")
        up_done, up_relu, h_ready, h_hi, h_lo = (
            sem("up_done"), sem("up_relu"), sem("h_ready"), sem("h_hi"), sem("h_lo"))
        dn_done, dn_added = sem("dn_done"), sem("dn_added")
        ln_scale, ln_scaled, f_ready, f_last = sem("ln_scale"), sem("ln_scaled"), sem("f_ready"), sem("f_last")
        s_out = sem("s_out")
        dve_own = sem("dve_own")

        x_tok = x.rearrange("a (t p) d -> (a t) p d", p=P)
        out_tok = out.rearrange("a (t p) d -> (a t) p d", p=P)
        w_in_v = w_in.rearrange("a (k p) e -> (a p) k e", p=P)
        wa_v = w_branch_a.rearrange("a (k p) e -> (a p) k e", p=P)
        wb_v = w_branch_b.rearrange("a (k p) e -> (a p) k e", p=P)
        wo_v = w_out.rearrange("a (k p) e -> (a k) p e", p=P)
        w1_v = w_ff1.rearrange("a (k p) f -> (a p) k f", p=P)
        w2_v = w_ff2.rearrange("a (k p) e -> (a k) p e", p=P)

        LOOPED = SB_GROUPS - 1

        def res_rows(tb):
            return res[:, :, bass.ds(tb * P, P)]

        def res_half(tb, h):
            return res[:, 4 * h:4 * h + 4, bass.ds(tb * P, P)]

        def by_block(ap, n=4):
            return ap.rearrange("p (k c) -> p k c", k=n)

        def apart(eng):
            eng.wait_ge(s_one, 1)

        def wait_stage(eng, g, roped):
            if roped:
                eng.wait_ge(rp_done, g * 4 - 12)
            else:
                eng.wait_ge(pj_plain, g * 6 + 4)
            if not (isinstance(g, int) and g == 0):
                eng.wait_ge(qk_done, g * 16)

        def wait_weights(eng, G, u):
            if G.sb:
                eng.wait_ge((a_even, a_odd)[u % 2], G.g * 8 + (u // 2 + 1))
            else:
                eng.wait_ge(a_ready, G.g * 8 + (u + 1 - 32))

        def tile_after(G, k):
            done = [i // 2 for i in G.halves_at(k) if i in (1, 3)]
            return done[0] if done else None

        def stack_part(G, k):
            if G.last:
                return None
            part = k - (19 if G.sb else 8)
            return part if 0 <= part < 3 else None

        def at_free(eng, G, k):
            g = G.g
            ends = [max(i for i, x in enumerate(G.batches) if x[0] == G.batches[i2][0]) == i2
                    for i2 in range(len(G.batches))]
            if k < 2:
                if not (isinstance(g, int) and g == 0):
                    eng.wait_ge(av_done, G.unit(0))
                return
            p = k - 2
            if ends[p]:
                eng.wait_ge(av_done, G.unit(sum(ends[:p])) + 1)
            else:
                per = sum(not e for e in ends)
                before = sum(not e for e in ends[:p])
                start = g * 8 if G.sb else g * 4 + 16
                eng.wait_ge(at_used, start + (before + 1))

        block = ctx.enter_context(nc.Block())

        @block.sync
        def _(sp):
            sp.dma_start(small[:, :, :], consts.rearrange("p (i c) -> p i c", i=4)).then_inc(s_const, 16)
            for b in range(2):
                sp.dma_start(y[:, b, :], x_tok[b]).then_inc(s_x[b], 16)

            def load_tile(n, col):
                if not (isinstance(n, int) and n == 0):
                    sp.wait_ge(wt_lo, n)
                sp.dma_start(w_raw[:, :, :], w_in_v[:, :, bass.ds(col, P)]).then_inc(wt_in, 16)

            for t in range(3):
                load_tile(t, SB_W * t)
                if t == 0:
                    for b in range(2, TB):
                        sp.dma_start(y[:, b, :], x_tok[b]).then_inc(s_x[b], 16)
            sp.dma_start(g_sub, subln_gain.rearrange("a d -> d a")).then_inc(s_lam, 16)
            for i, v in enumerate((lambda_q1, lambda_k1, lambda_q2, lambda_k2)):
                sp.dma_start(lams[:, i, :], v.broadcast_to([P, HD])).then_inc(s_lam, 16)
            with sp.Fori(1, SB_GROUPS) as g:
                for t in range(3):
                    load_tile(g * 3 + t, g * P + SB_W * t)
            sp.dma_start(cs[:, :, :], rope).then_inc(s_rope, 16)
            with sp.Fori(0, 4) as g:
                for t in range(3):
                    load_tile(g * 3 + (12 + t), g * P + SB_W * (3 + t))

            def load_branch(i):
                sp.wait_ge(wt_lo, i * 3 + 26)
                sp.dma_start(w_raw[:, 0:4, :], wa_v[:, :, bass.ds(i * P, P)]).then_inc(wt_in, 16)
                sp.dma_start(w_raw[:, 4:8, :], wb_v[:, :, bass.ds(i * P, P)]).then_inc(wt_in, 16)

            load_tile(24, GATE_A)
            load_tile(25, GATE_B)
            with sp.Fori(0, KT - 1) as i:
                load_branch(i)
                load_tile(i * 3 + 27, i * P + (GATE_A + P))
                load_tile(i * 3 + 28, i * P + (GATE_B + P))
            load_branch(KT - 1)

            sp.wait_ge(pj_done, 80)
            for k in range(KT):
                sp.dma_start(wo_raw[:, :, k, :], wo_v[k].rearrange("p (h c) -> p h c", h=2)).then_inc(wo_in[k], 16)

            def load_up(c, t, first=False):
                if not first:
                    sp.wait_ge(w1_lo, c * 2 + (t - 1))
                sp.dma_start(w1_raw[t][:, :, :], w1_v[:, :, bass.ds(c * 2 * P + t * P, P)]).then_inc(w1_in[t], 16)

            def load_down(c, t, first=False):
                if not first:
                    sp.wait_ge(w2_lo, c * 2 + (t - 1))
                sp.dma_start(w2_raw[t][:, :], w2_v[c * 2 + t]).then_inc(w2_in[t], 16)

            sp.wait_ge(m_ready, KT)
            for s in range(2):
                sp.dma_start(rows[s][:, :], x_tok[s]).then_inc(row_in[s], 16)
            sp.dma_start(gains[:, 0, :], ln1_gain.broadcast_to([P, D])).then_inc(s_gain1, 16)
            sp.wait_ge(wt_lo, 48)
            sp.dma_start(gains[:, 1, :], ln1_bias.broadcast_to([P, D])).then_inc(s_gain1, 16)
            for t in range(2):
                load_up(0, t, True)
            with sp.Fori(0, 3) as j:
                for s in range(2):
                    sp.wait_ge(x1_turned, j * 4 + (2 * s + 2))
                    sp.wait_ge(x1_kept, j * 2 + (s + 1))
                    sp.dma_start(rows[s][:, :], x_tok[j * 2 + (2 + s)]).then_inc(row_in[s], 16)

            sp.wait_ge(mt_lo, TB)
            sp.wait_ge(o_done, 2 * TB)
            for t in range(2):
                load_down(0, t, True)
            sp.wait_ge(x1_ready, TB)
            sp.dma_start(gains[:, 0, :], ln2_gain.broadcast_to([P, D])).then_inc(s_gain2, 16)
            sp.dma_start(gains[:, 1, :], ln2_bias.broadcast_to([P, D])).then_inc(s_gain2, 16)
            with sp.Fori(1, FC) as c:
                for t in range(2):
                    load_up(c, t)
                for t in range(2):
                    load_down(c, t)
            with sp.Fori(0, TB - 2) as tb:
                sp.wait_ge(f_ready, tb + 1)
                sp.dma_start(out_tok[tb], rows_out[:, bass.ds(tb, 1), :].rearrange("p a c -> p (a c)"))\
                  .then_inc(s_out, 16)
            for tb in (TB - 2, TB - 1):
                sp.wait_ge(f_last, tb - (TB - 3))
                sp.dma_start(out_tok[tb], rows_out[:, tb, :]).then_inc(s_out, 16)
            sp.wait_ge(s_out, 16 * TB)

        @block.tensor
        def _(pe):
            def half_matmuls(n_slot, h, last):
                o = p_proj[:, h, :]
                for k in range(KT):
                    cols = slice(h * NH, h * NH + NH)
                    pe.matmul(o, w_hi[n_slot][:, k, :], xt_h[:, k, cols], start=(k == 0), stop=False)
                    yield
                    pe.matmul(o, w_hi[n_slot][:, k, :], xt_l[:, k, cols], start=False, stop=False)
                    yield
                    mm = pe.matmul(o, w_lo[n_slot][:, k, :], xt_h[:, k, cols], start=False, stop=(k == KT - 1))
                    if k == KT - 1:
                        last(mm)
                    yield

            def filler(G):
                for t in range(G.tiles):
                    n = G.tile(t)
                    for h in range(2):
                        if h == 0:
                            pe.wait_ge(wt_lo, n + 1)
                        if t == 0:
                            pe.wait_ge(pj_plain, G.g * 6 + (5 + h) if G.sb else G.g * 2 + (17 + h))
                        elif G.rope:
                            pe.wait_ge(rp_free, G.roped(t - 1, h) + 1)
                        else:
                            pe.wait_ge(pj_plain, G.plain(t - 1, h) + 1)
                        yield from half_matmuls(t, h, lambda mm: mm.then_inc(pj_done, 1))

            def scores(g, j):
                m, qb = j % 2, j // 2
                width = (qb + 1) * P
                z = p_z[j % 2]
                if not (isinstance(g, int) and g == 0 and j < 2):
                    pe.wait_ge(z_read, g * 16 + (j - 1))
                lhs = q_st[m][:, qb * P:(qb + 1) * P]
                for lo in range(0, width, NH):
                    w = max(min(width - lo, NH), 256)
                    pe.matmul(z[:, lo:lo + w], lhs, k_hi[m][:, lo:lo + w], start=True, stop=False)
                    mm = pe.matmul(z[:, lo:lo + w], lhs, k_lo[m][:, lo:lo + w], start=False, stop=True)
                mm.then_inc(qk_done, 1)

            def first_scores(g):
                pe.wait_ge(st_act, g * 4 + 4)
                pe.wait_ge(st_dve, g * 4 + 4)
                pe.wait_ge(st_pool, g * 2 + 2)
                scores(g, 0)
                scores(g, 1)

            def square_sums(heads):
                for h in heads:
                    pe.wait_ge(z_read, 128)
                    pe.wait_ge(sq_ready, h + 1)
                    for b in range(TB):
                        mm = pe.matmul(p_z[1][:, 8 * h + b:8 * h + b + 1], squares[h][:, b * P:(b + 1) * P],
                                       one, start=True, stop=True)
                    mm.then_inc(ss_done, 1)

            def attention(G):
                g = G.g
                fill = filler(G)
                done = [0]

                def fill_to(n):
                    while done[0] < n:
                        next(fill)
                        done[0] += 1
                    if n == 48 * G.tiles:
                        for _ in fill:
                            raise AssertionError

                fill_to(12)
                scores(g, 2)
                fill_to(18)
                pe.wait_ge(pj_plain, g * 6 + 6 if G.sb else g * 2 + 18)
                for vb in range(2):
                    if not (isinstance(g, int) and g == 0 and vb == 0):
                        pe.wait_ge(tr_read, G.tr(vb))
                    for i in range(4):
                        blk = 4 * vb + i
                        mm = pe.transpose(p_tr[:, i * P:(i + 1) * P], stage[2][:, blk * P:(blk + 1) * P], ident)
                    mm.then_inc(tr_done, 1)
                    if vb == 0:
                        fill_to(24)
                        if not G.sb:
                            scores(g, 3)

                def turn(k):
                    u, b = G.batches[k]
                    qb = u // 2 if G.sb else u
                    if b == 0:
                        wait_weights(pe, G, u)
                    pe.wait_ge(tr_read, G.tr(k + 2))
                    first_blk, n, _ = span(qb, b)
                    for i in range(n):
                        blk = first_blk + i
                        w = sb_be[u % 4] if G.sb else df_e1[u % 3]
                        mm = pe.transpose(p_tr[:, i * P:(i + 1) * P], w[:, blk * P:(blk + 1) * P], ident)
                    mm.then_inc(tr_done, 1)

                def values(k):
                    u, b = G.batches[k]
                    qb = u // 2 if G.sb else u
                    first_blk, n, end = span(qb, b)
                    pe.wait_ge(tr_read, G.tr(k + 2) + 1)
                    if b == 0 and not (isinstance(g, int) and g == 0 and u == 0):
                        pe.wait_ge(av_read, G.unit(u))
                    for i in range(n):
                        blk = first_blk + i
                        if G.sb:
                            mm = pe.matmul(p_av[:, 0:256], v_st[:, blk, u % 2, :], a_t[:, k % 2, i, :, :],
                                           start=(blk == 0), stop=(blk == qb))
                        else:
                            mm = pe.matmul(p_av[:, 0:P], v_f[:, blk, :], w_t[:, k % 2, i * P:(i + 1) * P],
                                           start=(blk == 0), stop=(blk == qb))
                    mm.then_inc(av_done if end else at_used, 1)

                fill_to(G.head)
                for k, (u, b) in enumerate(G.batches):
                    last_b = k + 1 == len(G.batches) or G.batches[k + 1][0] != u
                    turn(k)
                    if k:
                        values(k - 1)
                    if G.sb:
                        if b == 0 and u + 3 < G.nunits:
                            scores(g, u + 3)
                    elif u + 2 < G.nunits:
                        if b == 0 and last_b:
                            before = G.until[k - 1] if k else G.head
                            fill_to(before + (G.until[k] - before) * 2 // 3)
                        if b == 0:
                            scores(g, 2 * u + 4)
                        if last_b:
                            scores(g, 2 * u + 5)
                    fill_to(G.until[k])
                if G.last:
                    square_sums(range(3))
                else:
                    first_scores(g + 1)
                values(len(G.batches) - 1)

            pe.wait_ge(s_const, 16)
            def turn_x(n):
                tb, j = n // 2, n % 2
                bank = x_banks[n % len(x_banks)]
                if j == 0:
                    pe.wait_ge(s_x[tb], 16)
                if n >= len(x_banks):
                    pe.wait_ge(xt_lo, n - len(x_banks) + 1)
                for i in range(4):
                    mm = pe.transpose(bank[:, i * P:(i + 1) * P],
                                      y[:, tb, (4 * j + i) * P:(4 * j + i + 1) * P], ident)
                mm.then_inc(xt_turned, 1)

            def first_half(t, h):
                if h == 0:
                    pe.wait_ge(wt_lo, t + 1)
                pe.wait_ge(xt_lo, TB * (h + 1))
                if t > 0:
                    pe.wait_ge(pj_plain, 2 * (t - 1) + h + 1)
                for _ in half_matmuls(t, h, lambda mm: mm.then_inc(pj_done, 1)):
                    pass

            for n in range(TB + 2):
                turn_x(n)
            pe.wait_ge(wt_lo, 1)
            pe.wait_ge(xt_lo, TB)
            n = TB + 2
            for i, _ in enumerate(half_matmuls(0, 0, lambda mm: mm.then_inc(pj_done, 1))):
                if i in (5, 11, 17):
                    turn_x(n)
                    turn_x(n + 1)
                    n += 2
            for t, h in ((0, 1), (1, 0), (1, 1), (2, 0), (2, 1)):
                first_half(t, h)
            pe.wait_ge(s_zero, 4)
            first_scores(0)
            attention(Group(0, True, 3, False))
            with pe.Fori(1, SB_GROUPS - 1) as g:
                attention(Group(g, True, 3, False))
            attention(Group(SB_GROUPS - 1, True, 3, True))
            attention(Group(SB_GROUPS, False, 3, True))
            with pe.Fori(SB_GROUPS + 1, GROUPS - 1) as g:
                attention(Group(g, False, 3, True))
            attention(Group(GROUPS - 1, False, 2, False))

            def branch(i, first, part, between=lambda: None):
                slot = 0 if isinstance(i, int) and i == KT - 1 else 2
                if part == 0:
                    pe.wait_ge(wt_lo, i * 3 + 27)
                for h in range(2):
                    if h == 1:
                        between()
                    if first:
                        pe.wait_ge(z_read, 128)
                    else:
                        pe.wait_ge(br_read, i * 2 + (part - 1))
                    o = p_z[part][:, h * NH:(h + 1) * NH]
                    for k in range(4 * part, 4 * part + 4):
                        cols = slice(h * NH, h * NH + NH)
                        pe.matmul(o, w_hi[slot][:, k, :], y_h[:, k, cols], start=(k % 4 == 0), stop=False)
                        pe.matmul(o, w_hi[slot][:, k, :], y_l[:, k, cols], start=False, stop=False)
                        mm = pe.matmul(o, w_lo[slot][:, k, :], y_h[:, k, cols], start=False, stop=(k % 4 == 3))
                mm.then_inc(br_done, 1)

            def gate(i, t):
                for h in range(2):
                    if h == 0:
                        pe.wait_ge(wt_lo, i * 3 + (28 + t))
                    pe.wait_ge(pj_plain, i * 4 + (35 + 2 * t + h))
                    yield from half_matmuls(t, h, lambda mm: mm.then_inc(pj_done, 1))

            def gates(i, tiles=range(2)):
                for t in tiles:
                    for _ in gate(i, t):
                        pass

            pe.wait_ge(ya_split, 4)
            branch(0, True, 0, lambda: square_sums([3]))
            next_gate = gate(0, 0)
            for h in range(4):
                for j in range(2):
                    n = 2 * h + j
                    for _ in range(4):
                        next(next_gate)
                    if n == 0:
                        pe.wait_ge(rs_ready, 1)
                        pe.wait_ge(tr_read, 160)
                        pe.wait_ge(av_read, 96)
                    if n >= 2:
                        pe.wait_ge(yn_ready, n - 1)
                    for i in range(4):
                        b = 4 * j + i
                        mm = pe.matmul((p_tr, p_av)[j][:, i * P:(i + 1) * P],
                                       rs[:, 8 * h + b:8 * h + b + 1].broadcast_to([P, P]), ident,
                                       start=True, stop=True)
                    mm.then_inc(bc_done, 1)
            for _ in next_gate:
                pass
            pe.wait_ge(yb_split, 4)
            branch(0, True, 1)
            gates(0, [1])
            with pe.Fori(1, KT - 2) as i:
                branch(i, False, 0)
                branch(i, False, 1)
                gates(i)
            gates(KT - 2)
            for i in (KT - 2, KT - 1):
                branch(i, False, 0)
                branch(i, False, 1)

            def project_out(tb, s):
                first = isinstance(tb, int) and tb == 0
                if first:
                    pe.wait_ge(mt_first_lo, 1)
                else:
                    pe.wait_ge(mt_lo, tb + 1)
                if isinstance(tb, int) and tb < 2:
                    pe.wait_ge(br_read, 2 * KT - 1 + tb)
                else:
                    pe.wait_ge(o_read, tb * 2 - 2)
                for h in range(2):
                    o = p_z[s][:, h * NH:(h + 1) * NH]
                    for k in range(KT):
                        if first and h == 0:
                            pe.wait_ge((wo_even, wo_odd)[k % 2], k // 2 + 1)
                            if k == KT - 1:
                                pe.wait_ge(mt_lo, 1)
                        pe.matmul(o, m_h[s][:, k, :], wo_h[:, h, k, :], start=(k == 0), stop=False)
                        pe.matmul(o, m_h[s][:, k, :], wo_l[:, h, k, :], start=False, stop=False)
                        mm = pe.matmul(o, m_l[s][:, k, :], wo_h[:, h, k, :], start=False, stop=(k == KT - 1))
                    mm.then_inc(o_done, 1)

            def turn_x1(tb, s):
                pe.wait_ge(x1_ready, tb + 1)
                for j in range(2):
                    if isinstance(tb, int) and tb == 0:
                        pe.wait_ge(pj_plain, 64)
                    else:
                        pe.wait_ge(x1_lo, tb * 2 + (j - 1))
                    for i in range(4):
                        blk = 4 * j + i
                        mm = pe.transpose(p_proj[:, j, i * P:(i + 1) * P], rows[s][:, blk * P:(blk + 1) * P], ident)
                    mm.then_inc(x1_turned, 1)

            project_out(0, 0)
            project_out(1, 1)

            def out_blocks(j):
                for s in range(2):
                    turn_x1(j * 2 + s, s)
                    project_out(j * 2 + (2 + s), s)

            out_blocks(0)
            with pe.Fori(1, TB // 2 - 1) as j:
                out_blocks(j)
            turn_x1(TB - 2, 0)

            def up(c, par, first=False):
                for h in range(2):
                    if first and h == 1:
                        pe.wait_ge(x1_lo, 2 * TB)
                    for t in range(2):
                        bank = 2 * h + t
                        if h == 0:
                            pe.wait_ge(w1_lo, c * 2 + (t + 1))
                        if first:
                            if t == 0:
                                pe.wait_ge(o_read, 2 * TB - 2 + 2 * h)
                            if t == 0 and h == 0:
                                pe.wait_ge(x1_lo, 8)
                            o = dn_banks[bank]
                        else:
                            o = up_banks[bank]
                            if isinstance(c, int) and c == 1:
                                pass
                            else:
                                pe.wait_ge(h_ready, c * 4 + (bank - 3))
                        w_h, w_l = w1_tiles(c, t)
                        for k in range(KT):
                            if first and (h, t, k) == (0, 1, 4):
                                turn_x1(TB - 1, 1)
                            cols = slice(h * NH, h * NH + NH)
                            pe.matmul(o, w_h[:, k, :], x1t_h[:, k, cols], start=(k == 0), stop=False)
                            pe.matmul(o, w_h[:, k, :], x1t_l[:, k, cols], start=False, stop=False)
                            mm = pe.matmul(o, w_l[:, k, :], x1t_h[:, k, cols], start=False, stop=(k == KT - 1))
                        mm.then_inc(up_done, 1)

            def down(c, par):
                for t in range(2):
                    pe.wait_ge(w2_lo, c * 2 + (t + 1))
                for tb in range(TB):
                    if tb % 4 == 0:
                        pe.wait_ge(h_lo, c * 4 + (2 + tb // 2))
                    for h in range(2):
                        n = 2 * tb + h
                        if isinstance(c, int) and c == 0 and n < 4:
                            pe.wait_ge(h_ready, n + 1)
                        else:
                            pe.wait_ge(dn_added, c * 16 + (n - 3))
                        o = dn_banks[n % 4]
                        for t in range(2):
                            rws = slice(tb * P, tb * P + P)
                            cols = slice(h * NH, h * NH + NH)
                            pe.matmul(o, h_h[par][t][:, rws], w2_h[t][:, cols], start=(t == 0), stop=False)
                            pe.matmul(o, h_h[par][t][:, rws], w2_l[t][:, cols], start=False, stop=False)
                            mm = pe.matmul(o, h_l[par][t][:, rws], w2_h[t][:, cols], start=False, stop=(t == 1))
                        mm.then_inc(dn_done, 1)

            up(0, 0, True)
            down(0, 0)
            up(1, 1)
            down(1, 1)
            with pe.Fori(1, FC // 2 - 1) as j:
                for par in range(2):
                    up(j * 2 + par, par)
                    down(j * 2 + par, par)
            up(FC - 2, 0)
            up(FC - 1, 1)
            for j in range(TB // 2):
                parts = [(n, c) for c in range(2) for n in range(4)] if j == 0 else \
                        [(4 * j + n, c) for n in range(4) for c in range(2)]
                for n, c in parts:
                    o = last_bank(n)
                    rws = slice(n // 2 * P, n // 2 * P + P)
                    cols = slice(n % 2 * NH, n % 2 * NH + NH)
                    if c == 0:
                        if n == 0:
                            pe.wait_ge(w2_lo, 2 * FC - 2)
                            pe.wait_ge(h_lo, 4 * FC - 4)
                        if n < 4:
                            pe.wait_ge(dn_added, (FC - 2) * 16 + (n - 3))
                        elif n < 8:
                            pe.wait_ge(h_ready, 4 * FC)
                        else:
                            pe.wait_ge(dn_added, (FC - 2) * 16 + (n - 7))
                    elif n == 0:
                        pe.wait_ge(w2_lo, 2 * FC)
                        pe.wait_ge(h_lo, 4 * FC)
                    for t in range(2):
                        w_h, w_l = ((w2_h[t], w2_l[t]), (w2_last_h[t], w2_last_l[t]))[c]
                        pe.matmul(o, h_h[c][t][:, rws], w_h[:, cols], start=(t + c == 0), stop=False)
                        pe.matmul(o, h_h[c][t][:, rws], w_l[:, cols], start=False, stop=False)
                        mm = pe.matmul(o, h_l[c][t][:, rws], w_h[:, cols], start=False, stop=(t + c == 2))
                    if c == 1:
                        mm.then_inc(dn_done, 1)

        @block.scalar
        def _(act):
            for n in range(2 * TB):
                tb, j = n // 2, n % 2
                act.wait_ge(xt_turned, n + 1)
                act.activation(xt_h[:, 4 * j:4 * j + 4, tb * P:(tb + 1) * P], by_block(x_banks[n % len(x_banks)]),
                               ACT.Copy).then_inc(xt_hi, 1)

            def plain(n, h, dst, wait_dst):
                act.wait_ge(pj_done, n * 2 + (h + 1))
                wait_dst()
                act.activation(dst[:, h * NH:(h + 1) * NH], p_proj[:, h, :], ACT.Copy).then_inc(pj_plain, 1)

            for t in range(2):
                for h in range(2):
                    plain(t, h, stage[t], lambda: None)

            def square(h):
                act.wait_ge(av_read, 8 * h + 72)
                if h == 2:
                    act.wait_ge(tr_done, 160 - len(DF_BATCH))
                if h == 3:
                    act.wait_ge(tr_done, 160)
                if h < 3:
                    act.wait_ge(qk_done, 128)
                act.activation(squares[h][:, :], y[:, 4 + h, :], ACT.Square).then_inc(sq_ready, 1)

            def stacks(g, roped, part):
                if part == 0:
                    wait_stage(act, g, roped)
                    for m in range(2):
                        r = slice(HD * m, HD * m + HD)
                        act.activation(q_st[m][r, :], stage[0][r, :], ACT.Copy).then_inc(st_act, 1)
                if part > 0:
                    m = part - 1
                    r, o = slice(HD * m, HD * m + HD), slice(HD * (1 - m), HD * (1 - m) + HD)
                    act.activation(k_hi[m][o, :], stage[1][r, :], ACT.Copy).then_inc(st_act, 1)

            def attention(G):
                g = G.g

                def project_done(k):
                    for i in ([0] if k < 0 else G.halves_at(k)):
                        t, h = i // 2, i % 2
                        if G.is_rope(t):
                            act.wait_ge(pj_done, G.tile(t) * 2 + (h + 1))
                            if not (isinstance(g, int) and g == SB_GROUPS - 1 and i == 0):
                                act.wait_ge(rp_done, G.roped(t, h))
                            for qd in range(4):
                                mm = act.activation(swap[32 * qd:32 * qd + 32, :],
                                                    p_proj[32 * (qd ^ 1):32 * (qd ^ 1) + 32, h, :], ACT.Copy)
                            mm.then_inc(rp_swap, 1)
                        else:
                            def free():
                                if t == 2:
                                    act.wait_ge(tr_done, G.tr(2))
                                else:
                                    act.wait_ge(st_act, g * 4 + 4)
                                    act.wait_ge(st_dve, g * 4 + 4)
                                    act.wait_ge(st_pool, g * 2 + 2)
                            plain(G.tile(t), h, stage[t], free)

                def weights_om(u):
                    qb = u // 2
                    act.wait_ge(qk_done, G.z(u) + 1)
                    if u < 4:
                        if not (isinstance(g, int) and g == 0) and u == 0:
                            act.wait_ge(tr_done, G.tr(0))
                    else:
                        wait_weights(act, G, u - 4)
                    act.activation(sb_om[u % 4][:, 0:(qb + 1) * P], p_z[u % 2][:, 0:(qb + 1) * P], ACT.Sigmoid,
                                   scale=-SCALE).then_inc(om_ready, 1)

                def weights_be(u):
                    qb = u // 2
                    if u >= 4:
                        last = max(k for k, x in enumerate(G.batches) if x[0] == u - 4)
                        act.wait_ge(tr_done, G.tr(last + 2) + 1)
                    act.activation(sb_be[u % 4][:, 0:(qb + 1) * P], p_z[u % 2][:, 0:(qb + 1) * P], ACT.Sigmoid,
                                   scale=SCALE).then_inc(z_read, 1)

                def exponentials(u, m):
                    act.wait_ge(pk_ready, G.z(2 * u + m) - 63)
                    if m == 0:
                        if u >= 3:
                            last = max(k for k, x in enumerate(G.batches) if x[0] == u - 3)
                            act.wait_ge(tr_done, G.tr(last + 2) + 1)
                        else:
                            act.wait_ge(tr_done, G.tr(0))
                            if u == 2:
                                act.wait_ge(av_done, G.unit(0))
                    act.activation((df_e1, df_e2)[m][u % 3][:, 0:(u + 1) * P], p_z[m][:, 0:(u + 1) * P], ACT.Exp,
                                   bias=n_peak[u % 2][:, m:m + 1], scale=SCALE,
                                   accum_out=e_sum[u % 2][:, m:m + 1]).then_inc(z_read, 1)

                def out_up(u):
                    if not G.sb:
                        apart(act)
                    act.wait_ge(av_done, G.unit(u) + 1)
                    if G.sb:
                        if not (isinstance(g, int) and g == 0 and u == 0):
                            act.wait_ge(av_read, G.unit(u))
                        act.activation(y_up[0:HD, :], p_av[HD:P, 0:256], ACT.Copy).then_inc(av_up, 1)
                    else:
                        act.activation(y[:, g, u * P:(u + 1) * P] if isinstance(g, int) else
                                       y[:, bass.ds(g, 1), u * P:(u + 1) * P].rearrange("p a c -> p (a c)"),
                                       p_av[:, 0:P], ACT.Copy).then_inc(av_read, 1)

                if G.sb:
                    for u in range(3):
                        weights_om(u)
                        weights_be(u)
                else:
                    for u, m in ((0, 0), (0, 1), (1, 0)):
                        exponentials(u, m)
                for vb in range(2):
                    act.wait_ge(tr_done, G.tr(vb) + 1)
                    if not (isinstance(g, int) and g == 0) and vb == 0:
                        act.wait_ge(av_done, G.unit(0))
                    if G.sb:
                        act.activation(v_st[:, 4 * vb:4 * vb + 4, :, 0:HD],
                                       p_tr[:, :].rearrange("p (b m d) -> p b m d", b=4, m=2),
                                       ACT.Copy).then_inc(tr_hi, 1)
                    else:
                        act.activation(v_f[:, 4 * vb:4 * vb + 4, :], by_block(p_tr[:, :]), ACT.Copy)\
                           .then_inc(tr_read, 1)
                        if vb == 0:
                            exponentials(1, 1)
                project_done(-1)
                scored = []
                for k, (u, b) in enumerate(G.batches):
                    qb = u // 2 if G.sb else u
                    _, n, last_b = span(qb, b)
                    act.wait_ge(tr_done, G.tr(k + 2) + 1)
                    at_free(act, G, k)
                    if G.sb:
                        act.activation(a_t[:, k % 2, 0:n, 0, :], by_block(p_tr[:, 0:n * P], n), ACT.Copy)\
                           .then_inc(tr_hi, 1)
                    else:
                        act.activation(w_t[:, k % 2, 0:n * P], p_tr[:, 0:n * P], ACT.Copy).then_inc(tr_read, 1)
                    if b == 0 and u > 0:
                        out_up(u - 1)
                    if G.sb:
                        if b == 0 and u + 3 < G.nunits:
                            weights_om(u + 3)
                        if last_b and u + 3 < G.nunits:
                            weights_be(u + 3)
                    else:
                        while scored:
                            exponentials(*scored.pop(0))
                        if u + 2 < G.nunits:
                            scored += [(u + 2, 0)] * (b == 0) + [(u + 2, 1)] * last_b
                    if G.last and 8 <= k < 11:
                        square(k - 8)
                    if stack_part(G, k) is not None:
                        stacks(g + 1, G.rope, stack_part(G, k))
                    project_done(k)
                out_up(G.nunits - 1)

            for part in range(3):
                stacks(0, False, part)
            for h in range(2):
                plain(2, h, stage[2], lambda: None)
            act.wait_ge(lam_dots, 1)
            act.activation(exps, dots, ACT.Exp).then_inc(lam_exps, 1)
            attention(Group(0, True, 3, False))
            with act.Fori(1, SB_GROUPS - 1) as g:
                attention(Group(g, True, 3, False))
            attention(Group(SB_GROUPS - 1, True, 3, True))
            attention(Group(SB_GROUPS, False, 3, True))
            with act.Fori(SB_GROUPS + 1, GROUPS - 1) as g:
                attention(Group(g, False, 3, True))
            attention(Group(GROUPS - 1, False, 2, False))

            square(3)
            act.wait_ge(v_eps, 1)
            act.activation(rs_t, rs_v, ACT.Sqrt).then_inc(v_root, 1)
            for h in range(4):
                act.wait_ge(yn_ready, 2 * h + 2)
                act.activation(y_h[:, 4 + h, :], y[:, 4 + h, :], ACT.Copy).then_inc(yb_hi, 1)
            for t in range(2):
                act.wait_ge(pj_plain, 34 + 2 * t)
                act.activation(stage[t][:, :], stage[t][:, :], ACT.Sigmoid).then_inc(gate_ready, 1)

            def gates(i, par):
                for t in range(2):
                    for h in range(2):
                        act.wait_ge(pj_done, i * 4 + (53 + 2 * t + h))
                        if h == 0 and not (isinstance(i, int) and i == 0):
                            act.wait_ge(m_ready, i)
                        act.activation(gate_pairs[par][t][:, h * NH:(h + 1) * NH], p_proj[:, h, :], ACT.Sigmoid)\
                           .then_inc(pj_plain, 1)

            gates(0, 1)
            with act.Fori(1, KT // 2 - 1) as j:
                gates(j * 2 - 1, 0)
                gates(j * 2, 1)
            gates(KT - 3, 0)
            gates(KT - 2, 1)

            def wo_high(k):
                act.wait_ge(wo_in[k], 16)
                act.activation(wo_h[:, :, k, :], wo_raw[:, :, k, :], ACT.Copy).then_inc(wo_hi, 1)

            def split_merged(tb, s):
                if isinstance(tb, int) and tb == 1:
                    act.wait_ge(br_done, 2 * KT)
                else:
                    apart(act)
                    act.wait_ge(o_done, tb * 2 - 2)
                act.activation(m_h[s][:, :, :], res_rows(tb), ACT.Copy).then_inc(mt_hi, 1)

            def norm(tb, s):
                act.wait_ge(ln_var, tb + 1)
                act.activation(ln_s[s], ln_v[s], ACT.Sqrt).then_inc(ln_root, 1)

            def keep(tb, s):
                apart(act)
                act.wait_ge(x1_ready, tb + 1)
                act.wait_ge(mt_lo, tb + 1)
                act.activation(res_rows(tb), by_block(rows[s][:, :], 8), ACT.Copy, scale=ALPHA)\
                   .then_inc(x1_kept, 1)

            def x1_high(tb):
                for j in range(2):
                    apart(act)
                    act.wait_ge(x1_turned, tb * 2 + (j + 1))
                    act.activation(x1t_h[:, 4 * j:4 * j + 4, bass.ds(tb * P, P)], by_block(p_proj[:, j, :]),
                                   ACT.Copy).then_inc(x1_hi, 1)

            last_k = KT - 1
            for k in range(4):
                wo_high(k)
            act.wait_ge(m_ready, last_k)
            act.activation(m_h[0][:, 0:last_k, :], res[:, 0:last_k, 0:P], ACT.Copy).then_inc(mt_first_hi, 1)
            for k in range(4, KT):
                wo_high(k)
            act.wait_ge(m_ready, KT)
            act.activation(m_h[0][:, last_k, :], res[:, last_k, 0:P], ACT.Copy).then_inc(mt_hi, 1)
            split_merged(1, 1)

            def out_blocks(j):
                for s in range(2):
                    split_merged(j * 2 + (2 + s), s)
                    norm(j * 2 + s, s)
                    keep(j * 2 + s, s)
                    x1_high(j * 2 + s)

            out_blocks(0)
            with act.Fori(1, TB // 2 - 1) as j:
                out_blocks(j)
            norm(TB - 2, 0)
            keep(TB - 2, 0)
            x1_high(TB - 2)
            norm(TB - 1, 1)

            def hidden(c, par, first=False):
                for n in range(4):
                    h, t = n // 2, n % 2
                    if first and n == 1:
                        x1_high(TB - 1)
                    if first and n == 2:
                        keep(TB - 1, 1)
                    o = (dn_banks if first else up_banks)[n]
                    act.wait_ge(up_done, c * 4 + (n + 1))
                    if not (first and n < 2):
                        act.wait_ge(h_ready, c * 4 + (n - 1))
                    act.activation(relu[:, n % 2, :], o, ACT.Relu).then_inc(up_relu, 1)
                    act.wait_ge(h_ready, c * 4 + (n + 1))
                    if not (isinstance(c, int) and c < 2) and n == 0:
                        act.wait_ge(dn_done, c * 16 - 16)
                    act.activation(h_h[par][t][:, h * NH:(h + 1) * NH], h_f[:, n % 2, :], ACT.Copy)\
                       .then_inc(h_hi, 1)

            hidden(0, 0, True)
            hidden(1, 1)
            with act.Fori(1, FC // 2) as j:
                hidden(j * 2, 0)
                hidden(j * 2 + 1, 1)
            with act.Fori(0, TB // 2 - 1) as j:
                for s in range(2):
                    norm(j * 2 + (TB + s), s)
                    apart(act)
                    act.wait_ge(ln_scale, j * 2 + (s + 1))
                    row = rows_out[:, bass.ds(j * 2 + s, 1), :].rearrange("p a c -> p (a c)")
                    act.activation(row, row, ACT.Copy, scale=ln_r[s]).then_inc(ln_scaled, 1)
            for s in range(2):
                norm(2 * TB - 2 + s, s)

        @block.vector
        def _(dve):
            own = Chain(dve, dve_own)

            def sub(o, a, b):
                return dve.tensor_tensor(o, a, b.bitcast(F32), ALU.subtract)

            dve.memset(one, 1.0).then_inc(s_one, 1)

            def split_tile(slot, arrived):
                dve.wait_ge(wt_in, arrived)
                dve.tensor_copy(w_hi[slot][:, :, :], w_raw[:, :, :]).then_inc(wt_hi, 1)

            def stacks(g, roped, part):
                rr = [slice(HD * m, HD * m + HD) for m in range(2)]
                if part == 0:
                    wait_stage(dve, g, roped)
                    for m in range(2):
                        dve.tensor_copy(k_hi[m][rr[m], :], stage[1][rr[m], :]).then_inc(st_dve, 1)
                if part > 0:
                    m = part - 1
                    dve.wait_ge(st_act, g * 4 + (m + 1))
                    sub(q_st[m][rr[1 - m], :], stage[0][rr[m], :], q_st[m][rr[m], :]).then_inc(st_dve, 1)

            for n in range(2 * TB):
                tb, j = n // 2, n % 2
                dve.wait_ge(xt_hi, n + 1)
                o = xt_l[:, 4 * j:4 * j + 4, tb * P:(tb + 1) * P]
                sub(o, by_block(x_banks[n % len(x_banks)]), xt_h[:, 4 * j:4 * j + 4, tb * P:(tb + 1) * P]).then_inc(xt_lo, 1)
                if n == 3:
                    split_tile(0, 16)
            split_tile(1, 32)
            split_tile(2, 48)
            dve.wait_ge(s_lam, 5 * 16)
            own(dve.tensor_tensor(lams[:, 0, :], lams[:, 0, :], lams[:, 1, :], ALU.mult))
            own.link(dve.tensor_tensor(lams[:, 2, :], lams[:, 2, :], lams[:, 3, :], ALU.mult))
            dve.tensor_reduce(dots, lams[:, 0::2, :], AX_X, ALU.add).then_inc(lam_dots, 1)
            own.link(dve.tensor_scalar(g_sub, g_sub, 1.0 - LAM_INIT, None, ALU.mult))
            dve.wait_ge(pj_done, 2)
            split_tile(0, 64)
            stacks(0, False, 0)
            dve.wait_ge(pj_done, 4)
            split_tile(1, 80)

            def split_output(t):
                if t == 0:
                    dve.wait_ge(y_done, 64)
                    dve.wait_ge(qk_done, 128)
                own.link(dve.tensor_copy(y_h[:, t, :], y[:, t, :]))
                sub(y_l[:, t, :], y[:, t, :], y_h[:, t, :]).then_inc(ya_split, 1)

            def attention(G):
                g = G.g

                def split_next(t):
                    n = G.tile(t)
                    dve.wait_ge(pj_done, n * 2 + 2)
                    last = G.last
                    split_tile(t, n * 16 + (16 * 4 + (16 if last else 0)))

                def rope_half(t, h):
                    cols = slice(h * NH, h * NH + NH)
                    dve.wait_ge(rp_swap, G.roped(t, h) + 1)
                    if t == 0 and h == 0:
                        dve.wait_ge(st_act, g * 4 + 4)
                        dve.wait_ge(st_dve, g * 4 + 4)
                        dve.wait_ge(st_pool, g * 2 + 2)
                        dve.wait_ge(s_rope, 16)
                    dve.tensor_tensor(stage[t][:, cols], p_proj[:, h, :], cs[:, 0, cols], ALU.mult)\
                       .then_inc(rp_free, 1)

                def rope_sum(t, h):
                    cols = slice(h * NH, h * NH + NH)
                    dve.wait_ge(rp_sin, G.roped(t, h) + 1)
                    dve.wait_ge(rp_free, G.roped(t, h) + 1)
                    dve.tensor_tensor(stage[t][:, cols], stage[t][:, cols], swap[:, :], ALU.add)\
                       .then_inc(rp_done, 1)

                def scans(u):
                    o, w = sb_om[u % 4], u // 2 * P
                    dg = o[:, w:w + P][:, ::-1]
                    dve.wait_ge(om_ready, G.unit(u) + 1)
                    scan = dve.tensor_tensor_scan(dg, dg, loose[:, ::-1], 1.0, ALU.mult, ALU.max)
                    if w:
                        own.link(scan)
                        rest = o[:, 0:w][:, ::-1]
                        scan = dve.tensor_tensor_scan(rest, rest, rest, o[:, w:w + 1], ALU.mult, ALU.bypass)
                    if u % 2:
                        scan.then_inc(om_odd, 1)
                    else:
                        scan.then_inc(om_even, 1)

                def product(u):
                    o, e, w = sb_om[u % 4], sb_be[u % 4], (u // 2 + 1) * P
                    if u % 2 == 0:
                        dve.wait_ge(om_even, G.g * 8 + (u // 2 + 1))
                        dve.wait_ge(be_masked, G.unit(u) + 1)
                        dve.tensor_tensor(e[:, 0:w - 1], e[:, 0:w - 1], o[:, 1:w], ALU.mult).then_inc(a_even, 1)

                def peaks(u, m):
                    s = u % 2
                    dve.wait_ge(qk_done, G.z(2 * u + m) + 1)
                    z = p_z[m]
                    dg = slice(u * P, (u + 1) * P)
                    own.link(dve.tensor_tensor(z[:, dg], z[:, dg], cap, ALU.min))
                    own.link(dve.tensor_reduce(peak[s][:, m:m + 1], z[:, 0:(u + 1) * P], AX_X, ALU.max))
                    dve.tensor_scalar(n_peak[s][:, m:m + 1], peak[s][:, m:m + 1], -SCALE, None, ALU.mult)\
                       .then_inc(pk_ready, 1)

                def combine(u):
                    s = u % 2
                    w = (u + 1) * P
                    dve.wait_ge(z_read, G.z(2 * u + 1) + 1)
                    own.link(dve.reciprocal(e_inv[s], e_sum[s]))
                    own.link(dve.tensor_tensor(c_neg[s][:, 0:1], e_inv[s][:, 1:2], n_lam, ALU.mult))
                    e1, e2 = df_e1[u % 3], df_e2[u % 3]
                    own.link(dve.tensor_scalar(e2[:, 0:w], e2[:, 0:w], c_neg[s][:, 0:1], None, ALU.mult))
                    dve.scalar_tensor_tensor(out=e1[:, 0:w], in0=e1[:, 0:w], scalar=e_inv[s][:, 0:1],
                                             in1=e2[:, 0:w], op0=ALU.mult, op1=ALU.add).then_inc(a_ready, 1)

                def out_low(u):
                    m, qb = u % 2, u // 2
                    dve.wait_ge(av_up, G.unit(u) + 1)
                    dve.tensor_tensor(y_sum[0:HD, :], p_av[0:HD, 0:256], y_up[0:HD, :], ALU.add)\
                       .then_inc(av_read, 1)

                def out_sum(u):
                    m, qb = u % 2, u // 2
                    dve.wait_ge(av_read, G.unit(u) + 1)
                    dst = (y[HD * m:HD * m + HD, g, qb * P:(qb + 1) * P] if isinstance(g, int) else
                           y[HD * m:HD * m + HD, bass.ds(g, 1), qb * P:(qb + 1) * P].rearrange("p a c -> p (a c)"))
                    dve.tensor_tensor(dst, y_sum[0:HD, 0:P], y_sum[0:HD, P:256], ALU.add).then_inc(y_done, 1)

                if G.sb:
                    for u in range(3):
                        scans(u)
                        if u < 2:
                            product(u)
                    for vb in range(2):
                        dve.wait_ge(tr_hi, g * 26 + (vb + 1))
                        sub(v_st[:, 4 * vb:4 * vb + 4, :, HD:P],
                            p_tr[:, :].rearrange("p (b m d) -> p b m d", b=4, m=2),
                            v_st[:, 4 * vb:4 * vb + 4, :, 0:HD]).then_inc(tr_read, 1)
                else:
                    for u in range(2):
                        for m in range(2):
                            peaks(u, m)
                        combine(u)
                to_sum, tile_due = [], None
                if G.is_rope(0):
                    rope_half(0, 0)
                    to_sum.append((0, 0))
                dve.wait_ge(pj_done, g * 6 + 6)
                split_tile(2, g * 48 + (16 * 6 + (16 if G.last else 0)))
                for k, (u, b) in enumerate(G.batches):
                    qb = u // 2 if G.sb else u
                    _, n, last_b = span(qb, b)
                    if not G.sb and to_sum:
                        rope_sum(*to_sum.pop())
                    if G.sb:
                        dve.wait_ge(tr_hi, g * 26 + (k + 3))
                        sub(a_t[:, k % 2, 0:n, 1, :], by_block(p_tr[:, 0:n * P], n), a_t[:, k % 2, 0:n, 0, :])\
                            .then_inc(tr_read, 1)
                        if b == 0 and u > 0:
                            out_low(u - 1)
                        if b == 0 and u + 2 < G.nunits:
                            product(u + 2)
                        if b == 0 and u > 0:
                            out_sum(u - 1)
                        if last_b and u + 3 < G.nunits:
                            scans(u + 3)
                    else:
                        if last_b and 0 < u < G.nunits - 1:
                            combine(u + 1)
                        if b == 0 and u + 2 < G.nunits:
                            peaks(u + 2, 0)
                        if last_b and u + 2 < G.nunits:
                            peaks(u + 2, 1)
                    if to_sum:
                        rope_sum(*to_sum.pop())
                    if G.last and k >= 8:
                        split_output(k - 8)
                    if stack_part(G, k) is not None:
                        stacks(g + 1, G.rope, stack_part(G, k))
                    for i in G.halves_at(k):
                        if G.is_rope(i // 2):
                            rope_half(i // 2, i % 2)
                            to_sum.append((i // 2, i % 2))
                    due_before, tile_due = tile_due, tile_after(G, k)
                    if G.sb:
                        due_before, tile_due = tile_due, None
                    if due_before is not None:
                        split_next(due_before)
                if tile_due is not None:
                    split_next(tile_due)
                if G.sb:
                    out_low(G.nunits - 1)
                    out_sum(G.nunits - 1)

            for part in (1, 2):
                stacks(0, False, part)
            dve.wait_ge(lam_exps, 1)
            own.link(dve.tensor_scalar(n_lam, exps[:, 1:2], -LAM_INIT, None, ALU.add))
            own.link(dve.tensor_tensor(n_lam, n_lam, exps[:, 0:1], ALU.subtract))
            attention(Group(0, True, 3, False))
            own.loop(1, SB_GROUPS - 1, 14, lambda g: attention(Group(g, True, 3, False)))
            attention(Group(SB_GROUPS - 1, True, 3, True))
            attention(Group(SB_GROUPS, False, 3, True))
            own.loop(SB_GROUPS + 1, GROUPS - 1, 56, lambda g: attention(Group(g, False, 3, True)))
            attention(Group(GROUPS - 1, False, 2, False))

            dve.wait_ge(av_done, 96)
            dve.wait_ge(ss_done, 4)
            dve.tensor_scalar(rs_v, p_z[1][:, 0:32], 1.0 / P, EPS, ALU.mult, ALU.add).then_inc(v_eps, 1)
            dve.wait_ge(v_root, 1)
            dve.wait_ge(v_eps, 1)
            own.link(dve.reciprocal(rs, rs_t))
            own.link(dve.tensor_tensor(ss, rs_v, rs, ALU.mult))
            own.link(dve.tensor_tensor(ss, ss, rs, ALU.mult))
            own.link(dve.tensor_scalar(ss, ss, -0.5, 1.5, ALU.mult, ALU.add))
            dve.tensor_tensor(rs, rs, ss, ALU.mult).then_inc(rs_ready, 1)
            for h in range(4):
                for j in range(2):
                    cols = slice(j * NH, j * NH + NH)
                    dve.wait_ge(bc_done, 2 * h + j + 1)
                    dve.wait_ge(sq_ready, h + 1)
                    dve.scalar_tensor_tensor(out=y[:, 4 + h, cols], in0=y[:, 4 + h, cols], scalar=g_sub,
                                             in1=(p_tr, p_av)[j][:, :], op0=ALU.mult, op1=ALU.mult)\
                        .then_inc(yn_ready, 1)
                dve.wait_ge(yb_hi, h + 1)
                sub(y_l[:, 4 + h, :], y[:, 4 + h, :], y_h[:, 4 + h, :]).then_inc(yb_split, 1)

            def merge(i, par, tiles, branch_next):
                gate = gate_pairs[par]
                for t in range(2):
                    dve.wait_ge(br_done, i * 2 + (t + 1))
                    if isinstance(i, int) and i == 0:
                        dve.wait_ge(gate_ready, t + 1)
                    else:
                        dve.wait_ge(pj_plain, i * 4 + (32 + 2 * t + 2))
                    dve.tensor_tensor(gate[t][:, :], gate[t][:, :], p_z[t][:, :], ALU.mult).then_inc(br_read, 1)
                dve.wait_ge(br_read, i * 2 + 2)
                dst = res[:, i, :] if isinstance(i, int) else \
                    res[:, bass.ds(i, 1), :].rearrange("p a c -> p (a c)")
                dve.tensor_tensor(dst, gate[0][:, :], gate[1][:, :], ALU.add).then_inc(m_ready, 1)
                if branch_next:
                    split_tile(2, i * 64 + (16 * (26 + 4 + 1)) + 16)
                for t in range(tiles):
                    dve.wait_ge(pj_done, i * 4 + (52 + 2 * t + 2))
                    split_tile(t, i * 64 + (16 * (31 + 2 + t)) + 0)

            merge(0, 0, 2, True)
            with dve.Fori(1, KT // 2 - 1) as j:
                merge(j * 2 - 1, 1, 2, True)
                merge(j * 2, 0, 2, True)
            merge(KT - 3, 1, 2, True)
            dve.wait_ge(pj_done, 78)
            split_tile(0, 896)
            merge(KT - 2, 0, 0, False)

            def merged_low(tb, s):
                dve.wait_ge(mt_hi, tb + 1)
                sub(m_l[s][:, :, :], res_rows(tb), m_h[s][:, :, :]).then_inc(mt_lo, 1)

            def wo_low(k):
                dve.wait_ge(wo_hi, k + 1)
                sub(wo_l[:, :, k, :], wo_raw[:, :, k, :], wo_h[:, :, k, :]).then_inc(wo_even, 1)

            last_k = KT - 1
            wo_low(0)
            wo_low(2)
            dve.wait_ge(mt_first_hi, 1)
            sub(m_l[0][:, 0:last_k, :], res[:, 0:last_k, 0:P], m_h[0][:, 0:last_k, :]).then_inc(mt_first_lo, 1)
            wo_low(4)
            wo_low(6)
            merge(KT - 1, 1, 0, False)
            dve.wait_ge(mt_hi, 1)
            sub(m_l[0][:, last_k, :], res[:, last_k, 0:P], m_h[0][:, last_k, :]).then_inc(mt_lo, 1)
            merged_low(1, 1)

            def layer_norm(row, tb, s, base_n, summed, scale_here):
                for h in range(2):
                    summed(h)
                    own(dve.bn_stats(stats[s][:, 6 * h:6 * h + 6], row[:, h * NH:(h + 1) * NH]))
                own.sync()
                dve.memset(ln_t[s], 0.0)
                own.link(dve.bn_aggr(aggr[s], stats[s]))
                dve.tensor_scalar(ln_v[s], aggr[s][:, 1:2], EPS, None, ALU.add).then_inc(ln_var, 1)
                own(dve.scalar_tensor_tensor(out=row, in0=row, scalar=aggr[s][:, 0:1],
                                             in1=gains[:, 0, :], op0=ALU.subtract, op1=ALU.mult))
                dve.wait_ge(ln_var, tb + (base_n + 1))
                dve.wait_ge(ln_root, tb + (base_n + 1))
                own.link(dve.reciprocal(ln_r[s], ln_s[s]))
                own.link(dve.scalar_tensor_tensor(out=ln_t[s], in0=ln_v[s], scalar=ln_r[s], in1=ln_r[s],
                                                  op0=ALU.mult, op1=ALU.mult))
                own.link(dve.tensor_scalar(ln_t[s], ln_t[s], -0.5, 1.5, ALU.mult, ALU.add))
                if not scale_here:
                    return dve.tensor_tensor(ln_r[s], ln_r[s], ln_t[s], ALU.mult)
                own.link(dve.tensor_tensor(ln_r[s], ln_r[s], ln_t[s], ALU.mult))
                return dve.scalar_tensor_tensor(out=row, in0=row, scalar=ln_r[s],
                                                in1=gains[:, 1, :], op0=ALU.mult, op1=ALU.add)

            def layer_norm1(tb, s, count):
                for h in range(2):
                    dve.wait_ge(o_done, tb * 2 + (h + 1))
                    if h == 0:
                        dve.wait_ge(row_in[s], count)
                    cols = slice(h * NH, h * NH + NH)
                    dve.scalar_tensor_tensor(out=rows[s][:, cols], in0=rows[s][:, cols], scalar=ALPHA,
                                             in1=p_z[s][:, cols], op0=ALU.mult, op1=ALU.add).then_inc(o_read, 1)
                layer_norm(rows[s][:, :], tb, s, 0, lambda h: dve.wait_ge(o_read, tb * 2 + (h + 1)), True)\
                    .then_inc(x1_ready, 1)

            def x1_low(tb):
                for j in range(2):
                    dve.wait_ge(x1_hi, tb * 2 + (j + 1))
                    cols = bass.ds(tb * P, P)
                    sub(x1t_l[:, 4 * j:4 * j + 4, cols], by_block(p_proj[:, j, :]), x1t_h[:, 4 * j:4 * j + 4, cols])\
                        .then_inc(x1_lo, 1)

            dve.wait_ge(s_gain1, 32)

            def out_blocks(j):
                for s in range(2):
                    layer_norm1(j * 2 + s, s, j * 16 + 16)
                    merged_low(j * 2 + (2 + s), s)
                    x1_low(j * 2 + s)

            out_blocks(0)
            own.loop(1, TB // 2 - 1, 16, out_blocks)
            layer_norm1(TB - 2, 0, 64)

            def up_high(c, t, first=False):
                if first:
                    if t == 0:
                        dve.wait_ge(o_done, 2 * TB - 1)
                elif t == 1 or not isinstance(c, int) or c < FC - 1:
                    dve.wait_ge(up_done, c * 4)
                dve.wait_ge(w1_in[t], c * 16 + 16)
                dve.tensor_copy(w1_tiles(c, t)[0][:, :, :], w1_raw[t][:, :, :]).then_inc(w1_hi, 1)

            def down_high(c, t, first=False):
                if not first:
                    dve.wait_ge(dn_done, c * 16)
                dve.wait_ge(w2_in[t], c * 16 + 16)
                dve.tensor_copy(w2_h[t][:, :], w2_raw[t][:, :]).then_inc(w2_hi, 1)

            def hidden(c, n, first=False):
                o = (dn_banks if first else up_banks)[n]
                dve.wait_ge(up_relu, c * 4 + (n + 1))
                if not (first and n < 2):
                    dve.wait_ge(h_lo, c * 4 + (n - 1))
                dve.scalar_tensor_tensor(out=h_f[:, n % 2, :], in0=o, scalar=0.0, in1=relu[:, n % 2, :],
                                         op0=ALU.max, op1=ALU.mult).then_inc(h_ready, 1)

            def hidden_low(c, par, n):
                h, t = n // 2, n % 2
                dve.wait_ge(h_hi, c * 4 + (n + 1))
                cols = slice(h * NH, h * NH + NH)
                sub(h_l[par][t][:, cols], h_f[:, n % 2, :], h_h[par][t][:, cols]).then_inc(h_lo, 1)

            def features(c, par, first=False):
                for n in range(4):
                    if first and n == 1:
                        x1_low(TB - 1)
                    hidden(c, n, first)
                    hidden_low(c, par, n)

            def add_rows(c, n):
                dve.wait_ge(dn_done, c * 16 + (n + 1))
                o = res[:, 4 * (n % 2):4 * (n % 2) + 4, (n // 2) * P:(n // 2 + 1) * P]
                dve.tensor_tensor(o, by_block(dn_banks[n % 4]), o, ALU.add).then_inc(dn_added, 1)

            up_high(0, 0, True)
            up_high(0, 1, True)
            x1_low(TB - 2)
            layer_norm1(TB - 1, 1, 64)
            dve.wait_ge(x1_kept, TB - 1)
            down_high(0, 0, True)
            down_high(0, 1, True)
            features(0, 0, True)

            def between(c):
                for t in range(2):
                    up_high(c + 1, t)
                for n in range(16):
                    add_rows(c, n)
                for t in range(2):
                    down_high(c + 1, t)

            dve.wait_ge(x1_kept, TB)
            between(0)
            features(1, 1)
            with dve.Fori(1, FC // 2 - 1) as j:
                for par in range(2):
                    between(j * 2 + (par - 1))
                    features(j * 2 + par, par)
            between(FC - 3)
            up_high(FC - 1, 0)
            features(FC - 2, 0)
            up_high(FC - 1, 1)
            for n in range(4):
                hidden(FC - 1, n)
                hidden_low(FC - 1, 1, n)
                if n == 1:
                    for t in range(2):
                        dve.wait_ge(w1_lo, 2 * FC)
                        dve.wait_ge(w2_in[t], FC * 16)
                        dve.tensor_copy(w2_last_h[t][:, :], w2_raw[t][:, :]).then_inc(w2_hi, 1)

            dve.wait_ge(s_gain2, 32)
            dve.wait_ge(up_done, 4 * FC)
            for tb in range(TB):
                s = tb % 2
                for h in range(2):
                    n = 2 * tb + h
                    dve.wait_ge(dn_done, 16 * (FC - 2) + n + 1)
                    dve.tensor_tensor(by_block(rows_out[:, tb, h * NH:(h + 1) * NH]), by_block(last_bank(n)),
                                      res_half(tb, h), ALU.add).then_inc(dn_added, 1)
                here = tb >= TB - 2
                done = layer_norm(rows_out[:, tb, :], tb, s, TB,
                                  lambda h: dve.wait_ge(dn_added, 16 * (FC - 2) + 2 * tb + (h + 1)), here)
                if here:
                    done.then_inc(f_last, 1)
                else:
                    done.then_inc(ln_scale, 1)

        @block.gpsimd
        def _(pool):
            for m in range(2):
                r = slice(HD * (1 - m), HD * (1 - m) + HD)
                pool.memset(k_lo[m][r, :].bitcast(F32), 0.0).then_inc(s_zero, 2)

            pool.wait_ge(s_zero, 4)

            def tile_low(n, slot):
                pool.wait_ge(wt_hi, n + 1)
                pool.tensor_tensor(w_lo[slot][:, :, :], w_raw[:, :, :], w_hi[slot][:, :, :].bitcast(F32),
                                   ALU.subtract).then_inc(wt_lo, 1)

            def sines(G, t, h):
                pool.wait_ge(rp_swap, G.roped(t, h) + 1)
                pool.tensor_tensor(swap[:, :], swap[:, :], cs[:, 1, h * NH:(h + 1) * NH], ALU.mult)\
                    .then_inc(rp_sin, 1)

            for t in range(4):
                tile_low(t, t % 3)

            def low_keys(g):
                pool.memset(idle, 0.0).then_inc(pool_idle, 1)
                pool.wait_ge(pool_idle, g + 1)
                for m in range(2):
                    r = slice(HD * m, HD * m + HD)
                    if m:
                        pool.wait_ge(st_pool, g * 2 + 1)
                    pool.wait_ge(st_dve, g * 4 + (m + 1))
                    pool.tensor_tensor(k_lo[m][r, :], stage[1][r, :], k_hi[m][r, :].bitcast(F32), ALU.subtract)\
                        .then_inc(st_pool, 1)
                pool.wait_ge(st_pool, g * 2 + 2)

            def mask(G, u):
                e = sb_be[u % 4][:, u // 2 * P:(u // 2 + 1) * P]
                pool.wait_ge(z_read, G.z(u) + 1)
                pool.tensor_tensor(e, e, strict, ALU.mult).then_inc(be_masked, 1)

            def product(G, u):
                o, e, w = sb_om[u % 4], sb_be[u % 4], (u // 2 + 1) * P
                pool.wait_ge(om_odd, G.g * 8 + (u // 2 + 1))
                pool.wait_ge(be_masked, G.unit(u) + 1)
                pool.tensor_tensor(e[:, 0:w - 1], e[:, 0:w - 1], o[:, 1:w], ALU.mult).then_inc(a_odd, 1)

            def attention(G):
                if G.sb:
                    for u in range(3):
                        mask(G, u)
                        if u == 1:
                            product(G, 1)
                if G.is_rope(0):
                    pool.wait_ge(s_rope, 16)
                    sines(G, 0, 0)
                tile_low(G.g * 3 + 5, 2)
                tile_due = None
                for k, (u, b) in enumerate(G.batches):
                    if G.sb and (k + 1 == len(G.batches) or G.batches[k + 1][0] != u):
                        if u % 2 and u + 2 < G.nunits:
                            product(G, u + 2)
                        if u + 3 < G.nunits:
                            mask(G, u + 3)
                    if stack_part(G, k) == 0:
                        low_keys(G.g + 1)
                    for i in G.halves_at(k):
                        if G.is_rope(i // 2):
                            sines(G, i // 2, i % 2)
                    due_before, tile_due = tile_due, tile_after(G, k)
                    if G.sb:
                        due_before, tile_due = tile_due, None
                    if due_before is not None:
                        tile_low(G.tile(due_before) + 3, due_before)
                if tile_due is not None:
                    tile_low(G.tile(tile_due) + 3, tile_due)

            low_keys(0)
            tile_low(4, 1)
            attention(Group(0, True, 3, False))
            with pool.Fori(1, SB_GROUPS - 1) as g:
                attention(Group(g, True, 3, False))
            attention(Group(SB_GROUPS - 1, True, 3, True))
            attention(Group(SB_GROUPS, False, 3, True))
            with pool.Fori(SB_GROUPS + 1, GROUPS - 1) as g:
                attention(Group(g, False, 3, True))
            attention(Group(GROUPS - 1, False, 2, False))
            with pool.Fori(0, KT - 2) as i:
                tile_low(i * 3 + 29, 2)
                tile_low(i * 3 + 30, 0)
                tile_low(i * 3 + 31, 1)
            tile_low(47, 0)

            for k in range(1, KT, 2):
                pool.wait_ge(wo_hi, k + 1)
                pool.tensor_tensor(wo_l[:, :, k, :], wo_raw[:, :, k, :], wo_h[:, :, k, :].bitcast(F32),
                                   ALU.subtract).then_inc(wo_odd, 1)

            def up_low(c, t):
                pool.wait_ge(w1_hi, c * 2 + (t + 1))
                high, low = w1_tiles(c, t)
                pool.tensor_tensor(low[:, :, :], w1_raw[t][:, :, :], high[:, :, :].bitcast(F32),
                                   ALU.subtract).then_inc(w1_lo, 1)

            def down_low(c, t):
                pool.wait_ge(w2_hi, c * 2 + (t + 1))
                pool.tensor_tensor(w2_l[t][:, :], w2_raw[t][:, :], w2_h[t][:, :].bitcast(F32),
                                   ALU.subtract).then_inc(w2_lo, 1)

            with pool.Fori(0, FC - 1) as c:
                for step in (up_low, down_low):
                    for t in range(2):
                        step(c, t)
            for t in range(2):
                up_low(FC - 1, t)
            for t in range(2):
                pool.wait_ge(w2_hi, 2 * FC - 1 + t)
                pool.tensor_tensor(w2_last_l[t][:, :], w2_raw[t][:, :], w2_last_h[t][:, :].bitcast(F32),
                                   ALU.subtract).then_inc(w2_lo, 1)
            with pool.Fori(0, TB - 2) as tb:
                row = rows_out[:, bass.ds(tb, 1), :].rearrange("p a c -> p (a c)")
                pool.wait_ge(ln_scaled, tb + 1)
                pool.tensor_tensor(row, row, gains[:, 1, :], ALU.add).then_inc(f_ready, 1)


_INS = ["x", "w_in", "w_branch_a", "w_branch_b", "w_out", "lambda_q1", "lambda_k1", "lambda_q2",
        "lambda_k2", "subln_gain", "ln1_gain", "ln1_bias", "w_ff1", "w_ff2", "ln2_gain", "ln2_bias"]


def kernel(**inputs):
    import numpy as _np
    import concourse.bacc as _bacc
    from concourse import mybir as _mybir
    from concourse.bass_utils import run_bass_kernel_spmd as _run

    nc = _bacc.Bacc("TRN2", target_bir_lowering=False, num_devices=1)
    arrays = {name: _np.ascontiguousarray(inputs[name]) for name in _INS}
    small, rope = const_arrays()
    arrays["consts"], arrays["rope"] = small, rope
    args = [nc.dram_tensor(name, a.shape, _mybir.dt.from_np(a.dtype), kind="ExternalInput").ap()
            for name, a in arrays.items()]
    args.append(nc.dram_tensor("out", (1, S, D), F32, kind="ExternalOutput").ap())
    layer_kernel(nc, *args)
    r = _run(nc, [arrays], core_ids=[0])
    return r.results[0]["out"]
```
